# Optimizing a Trainium2 kernel written in Bass

```python
import math
import jax, jax.numpy as jnp
from jax import lax
import numpy as np

D_MODEL = 2048
BATCH = 1
SEQ = 256
DEPTH = 4

N_MIXERS = 3
ROPE_THETA = 10000.0
EPS = 1e-6
NEG = -1e30

DA_QK_DIM = 128
DA_V_DIM = 2 * DA_QK_DIM
DA_HEADS = D_MODEL // DA_V_DIM
DA_WIDTH = DA_HEADS * DA_V_DIM
DA_QBLOCK = 128
DA_IN = 2 * DA_HEADS * DA_QK_DIM * 2 + DA_WIDTH + DA_WIDTH

SW_HEAD_DIM = 64
SW_Q_HEADS = D_MODEL // SW_HEAD_DIM
SW_KV_HEADS = SW_Q_HEADS // 8
SW_GROUP = SW_Q_HEADS // SW_KV_HEADS
SW_WIDTH = SW_Q_HEADS * SW_HEAD_DIM
WINDOW = 128
SW_IN = SW_WIDTH + 2 * SW_KV_HEADS * SW_HEAD_DIM + SW_WIDTH

ML_HEADS = 8
ML_V_DIM = D_MODEL // ML_HEADS
ML_QK_DIM = ML_V_DIM // 2
ML_WIDTH = ML_HEADS * ML_V_DIM
ML_CHUNK = 64
ML_IN = 2 * ML_HEADS * ML_QK_DIM + ML_WIDTH + ML_WIDTH + 2 * ML_HEADS + ML_WIDTH

N_A = (DEPTH + 2) // 3
N_B = (DEPTH + 1) // 3
N_C = DEPTH // 3

kernel_name = "hybrid_diffattn_swa_sink_mlstm_gated"

def rmsnorm(x, g):
    xf = x.astype(jnp.float32)
    y = xf * lax.rsqrt(jnp.mean(xf * xf, axis=-1, keepdims=True) + EPS)
    return (y * g.astype(jnp.float32)).astype(x.dtype)

def rope_tables(positions, dim):
    inv_freq = ROPE_THETA ** (-jnp.arange(0, dim, 2, dtype=jnp.float32) / dim)
    ang = positions.astype(jnp.float32)[..., None] * inv_freq
    return jnp.cos(ang)[:, :, None, :], jnp.sin(ang)[:, :, None, :]

def rope(x, cos, sin):
    half = x.shape[-1] // 2
    x1, x2 = x[..., :half], x[..., half:]
    return jnp.concatenate([x1 * cos - x2 * sin, x2 * cos + x1 * sin], axis=-1).astype(x.dtype)

def diff_attention(h, w_in, w_out, lam, subln_g, cos, sin, lambda_init):
    B, S, _ = h.shape
    H, d, dv = DA_HEADS, DA_QK_DIM, DA_V_DIM
    nq = 2 * H * d
    proj = h @ w_in
    q, k, v, g = jnp.split(proj, [nq, 2 * nq, 2 * nq + DA_WIDTH], axis=-1)
    q = rope(q.reshape(B, S, 2 * H, d), cos, sin) * (d ** -0.5)
    k = rope(k.reshape(B, S, 2 * H, d), cos, sin)
    q = q.reshape(B, S, H, 2, d).transpose(0, 2, 3, 1, 4)
    k = k.reshape(B, S, H, 2, d).transpose(0, 2, 3, 1, 4)
    v = v.reshape(B, S, H, dv).transpose(0, 2, 1, 3)
    lamf = lam.astype(jnp.float32)
    lam_full = (jnp.exp(jnp.sum(lamf[0] * lamf[1])) - jnp.exp(jnp.sum(lamf[2] * lamf[3])) + lambda_init)
    nb = S // DA_QBLOCK
    qb = q.reshape(B, H, 2, nb, DA_QBLOCK, d).transpose(3, 0, 1, 2, 4, 5)
    kpos = jnp.arange(S)

    def attend(args):
        qblk, blk = args
        s = jnp.einsum('bhmqd,bhmkd->bhmqk', qblk, k, preferred_element_type=jnp.float32)
        qpos = blk * DA_QBLOCK + jnp.arange(DA_QBLOCK)
        mask = kpos[None, :] <= qpos[:, None]
        p = jax.nn.softmax(jnp.where(mask, s, NEG), axis=-1)
        pd = p[:, :, 0] - lam_full * p[:, :, 1]
        return jnp.einsum('bhqk,bhkv->bhqv', pd.astype(v.dtype), v, preferred_element_type=jnp.float32)

    o = lax.map(attend, (qb, jnp.arange(nb)))
    o = o.transpose(1, 0, 3, 2, 4).reshape(B, S, H, dv)
    o = rmsnorm(o, subln_g) * (1.0 - lambda_init)
    o = o.reshape(B, S, DA_WIDTH) * jax.nn.silu(g.astype(jnp.float32))
    return o.astype(h.dtype) @ w_out

def sliding_window_attention(h, w_in, w_out, sinks, cos, sin):
    B, S, _ = h.shape
    d, KV, G, W = SW_HEAD_DIM, SW_KV_HEADS, SW_GROUP, WINDOW
    nkv = KV * d
    proj = h @ w_in
    q, k, v, g = jnp.split(proj, [SW_WIDTH, SW_WIDTH + nkv, SW_WIDTH + 2 * nkv], axis=-1)
    q = rope(q.reshape(B, S, SW_Q_HEADS, d), cos, sin) * (d ** -0.5)
    k = rope(k.reshape(B, S, KV, d), cos, sin)
    v = v.reshape(B, S, KV, d)
    nb = S // W
    qb = q.reshape(B, nb, W, KV, G, d)
    kb = k.reshape(B, nb, W, KV, d)
    vb = v.reshape(B, nb, W, KV, d)
    pad = ((0, 0), (1, 0), (0, 0), (0, 0), (0, 0))
    kk = jnp.concatenate([jnp.pad(kb, pad)[:, :-1], kb], axis=2)
    vv = jnp.concatenate([jnp.pad(vb, pad)[:, :-1], vb], axis=2)
    s = jnp.einsum('bnqhgd,bnkhd->bhgnqk', qb, kk, preferred_element_type=jnp.float32)
    qrel = jnp.arange(W)[:, None] + W
    krel = jnp.arange(2 * W)[None, :]
    band = (krel <= qrel) & (qrel - krel < W)
    has_prev = (jnp.arange(nb)[:, None, None] > 0) | (krel[None] >= W)
    mask = band[None] & has_prev
    s = jnp.where(mask[None, None, None], s, NEG)
    sk = sinks.astype(jnp.float32).reshape(KV, G)[None, :, :, None, None, None]
    m = jnp.maximum(jnp.max(s, axis=-1, keepdims=True), sk)
    e = jnp.exp(s - m)
    p = e / (jnp.sum(e, axis=-1, keepdims=True) + jnp.exp(sk - m))
    o = jnp.einsum('bhgnqk,bnkhd->bnqhgd', p.astype(vv.dtype), vv, preferred_element_type=jnp.float32)
    o = o.reshape(B, S, SW_WIDTH) * jax.nn.silu(g.astype(jnp.float32))
    return o.astype(h.dtype) @ w_out

def mlstm(h, w_in, b_gates, w_out, norm_g):
    B, S, _ = h.shape
    H, dk, dv, L = ML_HEADS, ML_QK_DIM, ML_V_DIM, ML_CHUNK
    nqk = H * dk
    proj = h @ w_in
    q, k, v, o, gif, g = jnp.split(
        proj, [nqk, 2 * nqk, 2 * nqk + ML_WIDTH, 2 * nqk + 2 * ML_WIDTH, 2 * nqk + 2 * ML_WIDTH + 2 * H], axis=-1)
    nc = S // L

    def chunks(t, dim):
        return t.reshape(B, nc, L, H, dim).transpose(1, 0, 3, 2, 4)

    qc = chunks(q * (dk ** -0.5), dk)
    kc = chunks(k, dk)
    vc = chunks(v, dv)
    gates = (gif.astype(jnp.float32) + b_gates.astype(jnp.float32)).reshape(B, S, 2, H)
    i_pre = gates[:, :, 0].reshape(B, nc, L, H).transpose(1, 0, 3, 2)
    log_f = jax.nn.log_sigmoid(gates[:, :, 1]).reshape(B, nc, L, H).transpose(1, 0, 3, 2)
    causal = jnp.tril(jnp.ones((L, L), dtype=bool))

    def step(carry, xs):
        C, n, m = carry
        qx, kx, vx, ix, fx = xs
        b = jnp.cumsum(fx, axis=-1)
        logw = jnp.where(causal, b[..., :, None] - b[..., None, :] + ix[..., None, :], NEG)
        log_inter = b + m[..., None]
        m_t = jnp.maximum(log_inter, jnp.max(logw, axis=-1))
        w_intra = jnp.exp(logw - m_t[..., None])
        w_inter = jnp.exp(log_inter - m_t)
        a = jnp.einsum('bhtd,bhsd->bhts', qx, kx, preferred_element_type=jnp.float32) * w_intra
        num = (jnp.einsum('bhts,bhsv->bhtv', a, vx)
               + w_inter[..., None] * jnp.einsum('bhvd,bhtd->bhtv', C, qx))
        den = jnp.sum(a, axis=-1) + w_inter * jnp.einsum('bhd,bhtd->bht', n, qx)
        hx = num / jnp.maximum(jnp.abs(den), jnp.exp(-m_t))[..., None]
        m_new = m_t[..., -1]
        wk = jnp.exp(b[..., -1:] - b + ix - m_new[..., None])
        decay = jnp.exp(b[..., -1] + m - m_new)
        C_new = decay[..., None, None] * C + jnp.einsum('bhs,bhsv,bhsd->bhvd', wk, vx, kx)
        n_new = decay[..., None] * n + jnp.einsum('bhs,bhsd->bhd', wk, kx)
        return (C_new, n_new, m_new), hx

    init = (jnp.zeros((B, H, dv, dk), jnp.float32), jnp.zeros((B, H, dk), jnp.float32),
            jnp.zeros((B, H), jnp.float32))
    _, hs = lax.scan(step, init, (qc, kc, vc, i_pre, log_f))
    hs = hs.transpose(1, 0, 3, 2, 4).reshape(B, S, H, dv)
    hs = rmsnorm(hs, norm_g).reshape(B, S, ML_WIDTH)
    out = hs * jax.nn.sigmoid(o.astype(jnp.float32)) * jax.nn.silu(g.astype(jnp.float32))
    return out.astype(h.dtype) @ w_out

def setup_inputs(seed: int = 0) -> dict:
    key = jax.random.key(seed)
    ks = jax.random.split(key, 16)
    f32 = jnp.float32
    nrm = lambda k, shape, s: jax.random.normal(k, shape, f32) * s
    x = jax.random.normal(ks[0], (BATCH, SEQ, D_MODEL), f32)
    positions = jnp.broadcast_to(jnp.arange(SEQ, dtype=jnp.int32), (BATCH, SEQ))
    norm_g = 1.0 + nrm(ks[1], (DEPTH, D_MODEL), 0.02)
    final_g = 1.0 + nrm(ks[2], (D_MODEL,), 0.02)
    da_w_in = nrm(ks[3], (N_A, D_MODEL, DA_IN), D_MODEL ** -0.5)
    da_w_out = nrm(ks[4], (N_A, DA_WIDTH, D_MODEL), DA_WIDTH ** -0.5)
    da_lambda = nrm(ks[5], (N_A, 4, DA_QK_DIM), 0.1)
    da_subln_g = 1.0 + nrm(ks[6], (N_A, DA_V_DIM), 0.02)
    sw_w_in = nrm(ks[7], (N_B, D_MODEL, SW_IN), D_MODEL ** -0.5)
    sw_w_out = nrm(ks[8], (N_B, SW_WIDTH, D_MODEL), SW_WIDTH ** -0.5)
    sw_sinks = nrm(ks[9], (N_B, SW_Q_HEADS), 0.5)
    ml_w_in = nrm(ks[10], (N_C, D_MODEL, ML_IN), D_MODEL ** -0.5)
    ib = nrm(ks[11], (N_C, ML_HEADS), 0.1)
    fb = 3.0 + nrm(ks[12], (N_C, ML_HEADS), 0.5)
    ml_b_gates = jnp.concatenate([ib, fb], axis=-1)
    ml_w_out = nrm(ks[13], (N_C, ML_WIDTH, D_MODEL), ML_WIDTH ** -0.5)
    ml_norm_g = 1.0 + nrm(ks[14], (N_C, ML_V_DIM), 0.02)
    return {"x": x, "positions": positions, "norm_g": norm_g, "final_g": final_g,
            "da_w_in": da_w_in, "da_w_out": da_w_out, "da_lambda": da_lambda, "da_subln_g": da_subln_g,
            "sw_w_in": sw_w_in, "sw_w_out": sw_w_out, "sw_sinks": sw_sinks,
            "ml_w_in": ml_w_in, "ml_b_gates": ml_b_gates, "ml_w_out": ml_w_out, "ml_norm_g": ml_norm_g}

def reference(x, positions, norm_g, final_g, da_w_in, da_w_out, da_lambda, da_subln_g,
              sw_w_in, sw_w_out, sw_sinks, ml_w_in, ml_b_gates, ml_w_out, ml_norm_g):
    cos_a, sin_a = rope_tables(positions, DA_QK_DIM)
    cos_b, sin_b = rope_tables(positions, SW_HEAD_DIM)
    for i in range(DEPTH):
        hn = rmsnorm(x, norm_g[i])
        kind, j = i % N_MIXERS, i // N_MIXERS
        if kind == 0:
            lambda_init = 0.8 - 0.6 * math.exp(-0.3 * i)
            y = diff_attention(hn, da_w_in[j], da_w_out[j], da_lambda[j], da_subln_g[j],
                               cos_a, sin_a, lambda_init)
        elif kind == 1:
            y = sliding_window_attention(hn, sw_w_in[j], sw_w_out[j], sw_sinks[j], cos_b, sin_b)
        else:
            y = mlstm(hn, ml_w_in[j], ml_b_gates[j], ml_w_out[j], ml_norm_g[j])
        x = x + y.astype(x.dtype)
    return rmsnorm(x, final_g)


_drawn_inputs = setup_inputs


def setup_inputs(seed=0):
    import zlib

    import numpy as np

    out = dict(_drawn_inputs(seed))
    spreads = {}
    factors = {'final_g': 2.766, 'da_subln_g': 4.482, 'sw_sinks': 5.723, 'ml_norm_g': 8.0}
    for name, (base, spread) in spreads.items():
        noise = np.random.default_rng([zlib.crc32(name.encode()), seed]).standard_normal(out[name].shape)
        drawn = base * np.exp(spread * noise) if base else spread * noise
        out[name] = __import__('jax').numpy.asarray(drawn.astype(out[name].dtype))
    for name, factor in factors.items():
        out[name] = (out[name] * factor).astype(out[name].dtype)
    return out
```

```python
import math
from contextlib import ExitStack

import numpy as np

import concourse.bass as bass
from concourse import mybir

P = 128
F32 = mybir.dt.float32
F32R = mybir.dt.float32r
I32 = mybir.dt.int32
ALU = mybir.AluOpType
ACT = mybir.ActivationFunctionType
AX_X = mybir.AxisListType.X

D = 2048
S = 256
T = S // P
KC = D // P
JW = 512
PAIRS = KC // 2
RING = 8
LAG = 4
ITERS = 4
EPS = 1e-6
NEG = -1e30
THETA = 10000.0
MAGIC = 12582912.0

LAYERS = [("da", 0), ("sw", 0), ("ml", 0), ("da", 1)]
NL = len(LAYERS)
HEAD_JOBS = {"da": 0, "sw": 1, "ml": 0}
ITER_JOBS = {"da": 4, "sw": 2, "ml": 4}
OUT_JOBS = D // JW
BLK = 3 * P

DA = dict(q_evac=11, q_T=10, q_copy=14, k_evac=19, k_T=18, k_copy=22, v_evac=27,
          score=20, softmax=24, diff=(26, 28), p_T=(24, 26), p_copy=(28, 30), pv=(26, 28), ssq=(30, 32),
          g_tanh=35, gate=36, mix=37, o_T=35, o_split=39)
SW = dict(kv_evac=3, k_stage=10, v_stage=12, k_T=9, k_copy=13, q_evac=11, q_T=10, q_copy=14,
          score=12, softmax=16, p_T=14, p_copy=18, pv=16, pv7=23, sink=(20, 24), den=(22, 26),
          g_tanh=19, gate=20, mix=(23, 27), o_T=(21, 25), o_split=(25, 29))
SW_LAST = dict(pv7=22, mix=(23, 26), o_T=(21, 22), o_split=(25, 26))
ML = dict(qk_evac=11, qk_T=15, qk_copy=19, score=(17, 18), decay=(17, 18), weigh=(21, 22),
          v_evac=19, pv=(20, 21), den=25, ssq=26, comb=29, o_tanh=27,
          g_tanh=35, gate=36, mix=37, o_T=35, o_split=39)

COUNTS = {
    "tp_0":      ((1, 0, 4), (0, 4, 4), (0, 6, 4), (4, 3, 4)),
    "tp_1":      ((0, 0, 4), (0, 4, 4), (0, 6, 4), (4, 2, 4)),
    "sc_0":      ((0, 0, 0), (0, 3, 0), (0, 8, 0), (0, 2, 0)),
    "sc_1":      ((0, 0, 0), (0, 3, 0), (0, 3, 0), (0, 2, 0)),
    "t_hi":      ((0, 0, 16), (0, 4, 16), (0, 4, 16), (0, 4, 16)),
    "x_sq":      ((0, 0, 8), (0, 0, 8), (0, 0, 8), (0, 0, 8)),
    "roped":     ((0, 0, 0), (0, 4, 0), (2, 2, 0), (0, 0, 0)),
    "k_staged":  ((0, 0, 0), (0, 0, 0), (0, 1, 0), (0, 0, 0)),
    "v_staged":  ((0, 0, 0), (0, 0, 0), (0, 1, 0), (0, 0, 0)),
    "neg_max":   ((0, 0, 0), (0, 4, 0), (0, 8, 0), (0, 0, 0)),
    "decay_arg": ((0, 0, 0), (0, 0, 0), (0, 0, 0), (0, 2, 0)),
    "exp_done":  ((0, 0, 0), (0, 8, 0), (0, 16, 0), (0, 2, 0)),
    "diff_done": ((0, 0, 0), (0, 4, 0), (0, 0, 0), (0, 0, 0)),
    "sink_arg":  ((0, 0, 0), (0, 0, 0), (0, 2, 0), (0, 0, 0)),
    "sink_exp":  ((0, 0, 0), (0, 0, 0), (0, 2, 0), (0, 0, 0)),
    "den_inv":   ((0, 0, 0), (0, 0, 0), (0, 0, 0), (0, 1, 0)),
    "ssq_done":  ((0, 0, 0), (0, 4, 0), (0, 0, 0), (0, 4, 0)),
    "o_rstd":    ((0, 0, 0), (0, 2, 0), (0, 0, 0), (0, 1, 0)),
    "tanh_done": ((0, 0, 0), (0, 2, 0), (0, 2, 0), (0, 2, 0)),
}
KINDS = ("start", "da", "sw", "ml")


def _bases():
    kinds = ["start"] + [k for k, _ in LAYERS]
    out = {}
    for name, by_kind in COUNTS.items():
        at, n = {}, 0
        for l, kind in enumerate(kinds):
            at[l - 1] = n
            head, per, tail = by_kind[KINDS.index(kind)]
            n += head + per * ITERS + tail
        out[name] = at
    return out


BASE = _bases()


def _counts(l, name):
    return COUNTS[name][KINDS.index("start" if l < 0 else LAYERS[l][0])]


def in_head(l, name, n):
    return BASE[name][l] + n


def in_iter(l, name, i, n):
    head, per, _ = _counts(l, name)
    return i * per + (BASE[name][l] + head + n)


def in_out(l, name, n):
    head, per, _ = _counts(l, name)
    return BASE[name][l] + head + per * ITERS + n


def _jobs():
    first, loop, out, by = [], [], [], []
    for kind, _ in LAYERS:
        first.append(len(by))
        by += ["act"] * HEAD_JOBS[kind]
        loop.append(len(by))
        by += (["act"] * (ITER_JOBS[kind] - 1) + ["dve"]) * ITERS
        out.append(len(by))
        by += ["dve"] * OUT_JOBS
    return first, loop, out, by


JOB0, LOOP0, OUT0, EMPTIED_BY = _jobs()
NJOBS = len(EMPTIED_BY)
J0_LAST = NJOBS - 1


def emptied(l, j, i=0):
    who = EMPTIED_BY[j]
    per = ITER_JOBS[LAYERS[l][0]]
    in_loop = LOOP0[l] <= j < OUT0[l]
    step = 2 * sum(w == who for w in EMPTIED_BY[LOOP0[l]:LOOP0[l] + per]) if in_loop else 0
    return who, i * step + 2 * sum(w == who for w in EMPTIED_BY[:j + 1])


class Own:

    def __init__(self, eng, sem):
        self.eng, self.sem, self.n, self.more = eng, sem, 0, 0

    def step(self, instruction):
        instruction.then_inc(self.sem, 1)
        self.n += 1

    def wait(self):
        self.eng.wait_ge(self.sem, self.more + self.n)

    def enter(self, i, per):
        self.at, self.per = self.n, per
        self.more = (i - 1) * per

    def leave(self):
        assert self.n - self.at == self.per, (self.n - self.at, self.per)
        self.n += (ITERS - 2) * self.per
        self.more = 0


OWN_STEPS = {
    ("dve", "da"): 26, ("dve", "sw"): 26, ("dve", "ml"): 7,
    ("pool", "da"): 4, ("pool", "sw"): 0, ("pool", "ml"): 2,
}


class Place:

    def __init__(self, l, phase, i, idx):
        self.l, self.kind, self.phase, self.i, self.idx = l, LAYERS[l][0], phase, i, idx
        self.period = PAIRS * ITER_JOBS[self.kind]
        self.first = isinstance(i, int)
        self.start = l == 0 and phase == "iter" and self.first

    def due(self, when):
        if self.phase == "iter" and when == self.idx:
            return self.i
        if self.phase == "iter" and when == self.idx + self.period and not self.first:
            return self.i - 1
        if self.phase == "out" and when == self.idx + self.period:
            return ITERS - 1
        return None

    def x_due(self, when):
        n, at = divmod(self.idx, PAIRS)
        if self.phase == "out":
            return (self.l, n - 1) if at == when and n >= 1 else None
        opening = self.phase == "head" or (self.phase == "iter" and self.first and not HEAD_JOBS[self.kind])
        return (self.l - 1, OUT_JOBS - 1) if opening and self.idx == when and self.l > 0 else None


def sw_at(w, name):
    return SW_LAST[name] if w.phase == "out" else SW[name]


def walk(eng, l, pair, own=None, who=None):
    kind = LAYERS[l][0]
    nj = ITER_JOBS[kind]
    for p in range(PAIRS * HEAD_JOBS[kind]):
        pair(Place(l, "head", None, p), JOB0[l], 0, 0, p)
    for j in range(nj):
        for p in range(PAIRS):
            pair(Place(l, "iter", 0, j * PAIRS + p), LOOP0[l] + j, 0, j, p)
    with eng.Fori(1, ITERS) as i:
        if own:
            own.enter(i, OWN_STEPS[who, kind])
        for j in range(nj):
            for p in range(PAIRS):
                pair(Place(l, "iter", i, j * PAIRS + p), LOOP0[l] + j, i, j, p)
        if own:
            own.leave()
    for j in range(OUT_JOBS):
        for p in range(PAIRS):
            pair(Place(l, "out", None, j * PAIRS + p), OUT0[l] + j, 0, j, p)


def build(nc, x, positions, norm_g, final_g, da_w_in, da_w_out, da_lambda, da_subln_g, sw_w_in, sw_w_out,
          sw_sinks, ml_w_in, ml_b_gates, ml_w_out, ml_norm_g, freqs, out):
    ctx = ExitStack()
    with ctx:
        def sb(name, shape, dt=F32):
            return ctx.enter_context(nc.sbuf_tensor(name, shape, dt))

        def sem(name):
            return ctx.enter_context(nc.semaphore(name))

        xres = sb("xres", [P, T, D])
        xt_hi, xt_lo = sb("xt_hi", [P, KC, S], F32R), sb("xt_lo", [P, KC, S], F32R)
        ot_hi, ot_lo = sb("ot_hi", [P, KC, S], F32R), sb("ot_lo", [P, KC, S], F32R)
        raw = sb("raw", [P, KC, JW])
        w_hi, w_lo = sb("w_hi", [P, RING, JW], F32R), sb("w_lo", [P, RING, JW], F32R)
        qs, vs, gs = (sb(n, [P, T, JW]) for n in ("qs", "vs", "gs"))
        shared = sb("shared", [P, D])
        ks = shared[:, 0:T * JW].rearrange("p (t n) -> p t n", t=T)
        rope_a, rope_b = shared[:, 2 * JW:3 * JW], shared[:, 3 * JW:4 * JW]
        ang = shared[:, 0:T * 96].rearrange("p (t n) -> p t n", t=T)
        turns_flat, red_flat = (shared[:, 512 * n:512 * n + 2 * T * 96] for n in (1, 2))
        turns, red = (a.rearrange("p (a t n) -> p a t n", a=2, t=T) for a in (turns_flat, red_flat))
        wide = shared[:].rearrange("p (h n) -> p h n", h=8)
        th = sb("th", [P, T, JW])
        qT, kT = sb("qT", [P, 4, S]), sb("kT", [P, 4, S])
        scr = sb("scr", [P, 8, BLK])
        scr_flat = scr[:].rearrange("p a b -> p (a b)")
        pT = sb("pT", [P, 2, BLK])
        junk_o, junk_x = sb("junk_o", [P, S]), sb("junk_x", [P, JW])
        ident, ones = sb("ident", [P, P]), sb("ones", [P, P])
        tri = sb("tri", [P, P])
        masks = sb("masks", [P, 4 * P])
        mask_causal, mask_da, mask_sw = masks[:, P:2 * P], masks[:, 0:2 * P], masks[:, 2 * P:4 * P]
        mask_ml = sb("mask_ml", [P, P])
        half_pow, eps_t = sb("half_pow", [P, 4]), sb("eps_t", [P, 4])
        inv_width = {n: sb(f"inv_{n}", [P, 4]) for n in (S, D)}
        rows = sb("rows", [P, P])
        gcol = sb("gcol", [P, NL * KC + 6])
        cos_a, sin_a = sb("cos_a", [P, T, 64]), sb("sin_a", [P, T, 2, 64])
        cos_b, sin_b = sb("cos_b", [P, T, 32]), sb("sin_b", [P, T, 2, 32])
        pos_i, pos_f = sb("pos_i", [P, T], I32), sb("pos_f", [P, T])
        freq = sb("freq", [P, 96])
        lam_s, lam = sb("lam_s", [P, 2, 2]), sb("lam", [P, 2])
        sinks, sink_cur = sb("sinks", [P, 32]), sb("sink_cur", [P, 8])
        k_stage, v_stage = sb("k_stage", [P, T, 2, 64]), sb("v_stage", [P, T, 64])
        row_max, neg_max_t = sb("row_max", [P, 8, T]), sb("neg_max_t", [P, 8, T])
        exp_sum, exp_inv = sb("exp_sum", [P, 8, T]), sb("exp_inv", [P, 8, T])
        sink_t = sb("sink_t", [P, 8, T])
        x_ss, x_sum, x_ms = sb("x_ss", [P, T, 4]), sb("x_sum", [P, T]), sb("x_ms", [P, T])
        rstd, rstd_half = sb("rstd", [P, T]), sb("rstd_half", [P, T])
        o_ss, o_ms, o_rs = sb("o_ss", [P, 2, T]), sb("o_ms", [P, 2, T]), sb("o_rs", [P, 2, T])
        den_s, den_i, comb = sb("den_s", [P, 2, T]), sb("den_i", [P, 2, T]), sb("comb", [P, 2, T])
        wg_raw = sb("wg_raw", [P, KC, 16])
        wg_hi, wg_lo = sb("wg_hi", [P, KC, 16], F32R), sb("wg_lo", [P, KC, 16], F32R)
        gbias, gz = sb("gbias", [P, 16]), sb("gz", [P, T, 16])
        lf_a, lf_e, lf_u, lf_l = (sb(n, [P, T, 8]) for n in ("lf_a", "lf_e", "lf_u", "lf_l"))
        lf = sb("lf", [P, T, 8])
        F_t = sb("F_t", [P, 3, 8])
        rcol = sb("rcol", [P, 3, 8])
        PAD = 64
        vs_row, gs_row = (a[0:8].rearrange("p t n -> p (t n)") for a in (vs, gs))
        RUN = T * (PAD + P)
        run_a, run_b = (vs_row[:, RUN * n:RUN * n + RUN].rearrange("p (t n) -> p t n", t=T) for n in range(2))
        F_r, m_r = (gs_row[:, S * n:S * n + S].rearrange("p (t n) -> p t n", t=T) for n in range(2))
        m_end = sb("m_end", [8, 1])
        exp_nm = sb("exp_nm", [P, T, 8])

        def bank(name):
            return ctx.enter_context(nc.psum_tensor(name, [P, 512], F32))

        acc = [[bank(f"acc{b}{t}") for t in range(T)] for b in range(2)]
        tp = [bank(f"tp{b}") for b in range(2)]
        sc = [bank(f"sc{b}") for b in range(2)]

        raw_full = [sem(f"raw_full{s}") for s in range(4)]
        raw_half = [sem(f"raw_half{s}") for s in range(4)]
        hi_ready, lo_ready = sem("hi_ready"), sem("lo_ready")
        pairs_done = sem("pairs_done")
        act_emptied, dve_emptied = sem("act_emptied"), sem("dve_emptied")
        full = {n: sem(n + "_full") for n in ("tp_0", "tp_1", "sc_0", "sc_1")}
        free = {n: sem(n + "_free") for n in ("tp_0", "tp_1", "sc_0", "sc_1")}
        sig = {n: sem(n) for n in COUNTS if n not in full}
        tiles_done = sem("tiles_done")
        x_summed, rstd_ready = sem("x_summed"), sem("rstd_ready")
        dve_own, act_started, pool_own = sem("dve_own"), sem("act_started"), sem("pool_own")
        scores_seen = sem("scores_seen")
        gate_dve, gate_act = sem("gate_dve"), sem("gate_act")
        x_in = [sem(f"x_in{n}") for n in range(OUT_JOBS)]
        gains_in, small_in, wg_in, final_in = sem("gains_in"), sem("small_in"), sem("wg_in"), sem("final_in")
        consts, tables, angles = sem("consts"), sem("tables"), sem("angles")
        y_gained, y_ready, y_act, stored = sem("y_gained"), sem("y_ready"), sem("y_act"), sem("stored")
        SMALL = 16 * 6

        block = ctx.enter_context(nc.Block())

        def wait_emptied(eng, l, j, i=0):
            who, value = emptied(l, j, i)
            eng.wait_ge(act_emptied if who == "act" else dve_emptied, value)

        def scale_col(l, c2):
            kind, j = LAYERS[l]
            at = NL * KC + {"da": 2 * j, "ml": 4}.get(kind, 0) + c2
            return None if kind == "sw" else gcol[:, at:at + 1]

        @block.sync
        def _(sp):
            def load_x(n):
                cols = slice(JW * n, JW * n + JW)
                sp.dma_start(xres[:, :, cols], x[0, :, cols].rearrange("(t p) n -> p t n", p=P)).then_inc(x_in[n], 16)

            sp.dma_start(rows[0:64, :], norm_g.rearrange("l (c p) -> (l c) p", p=P)).then_inc(gains_in, 16)
            sp.dma_start(rows[64:68, :], da_subln_g.rearrange("l (c p) -> (l c) p", p=P)).then_inc(gains_in, 16)
            sp.dma_start(rows[68:70, :], ml_norm_g.rearrange("l (c p) -> (l c) p", p=P)).then_inc(gains_in, 16)

            def load_small():
                def small(dst, src):
                    sp.dma_start(dst, src).then_inc(small_in, 16)

                for t in range(T):
                    small(pos_i[:, t:t + 1], positions[0, P * t:P * t + P].rearrange("(p a) -> p a", a=1))
                small(freq[:], freqs.rearrange("(a n) -> a n", a=1).to_broadcast([P, 96]))
                small(scr_flat[:, 0:1024],
                      da_lambda.rearrange("l a n -> (l a n)").rearrange("(a n) -> a n", a=1).to_broadcast([P, 1024]))
                small(sinks[:], sw_sinks.to_broadcast([P, 32]))
                small(gbias[:], ml_b_gates.to_broadcast([P, 16]))

            def load(w, col, J, opening, pair_of=0):
                for s in range(4):
                    if opening:
                        load_x(s)
                    else:
                        sp.wait_ge(lo_ready, PAIRS * (J - 1) + 2 * s + 2)
                    rows_of = w[512 * s:512 * s + 512, :].rearrange("(k p) n -> p k n", p=P)
                    if pair_of:
                        half = JW // 2
                        for a, arrived in enumerate((raw_half, raw_full)):
                            sp.dma_start(raw[:, 4 * s:4 * s + 4, half * a:half * a + half],
                                         rows_of[:, :, bass.ds(col + pair_of * a, half)]).then_inc(arrived[s], 16)
                    else:
                        sp.dma_start(raw[:, 4 * s:4 * s + 4, :], rows_of[:, :, bass.ds(col, JW)])\
                          .then_inc(raw_full[s], 16)

            for l, (kind, n) in enumerate(LAYERS):
                w_in = {"da": da_w_in, "sw": sw_w_in, "ml": ml_w_in}[kind][n]
                w_out = {"da": da_w_out, "sw": sw_w_out, "ml": ml_w_out}[kind][n]

                def iteration(i):
                    J = LOOP0[l] + ITER_JOBS[kind] * i
                    opening = l == 0 and isinstance(i, int)
                    if kind == "da":
                        for j in range(4):
                            load(w_in, D * j + JW * i, J + j, opening and j == 0)
                            if opening and j == 0:
                                load_small()
                    elif kind == "sw":
                        load(w_in, JW * i, J, False)
                        load(w_in, D + JW + JW * i, J + 1, False)
                    else:
                        load(w_in, JW // 2 * i, J, False, pair_of=D // 2)
                        load(w_in, D + JW * i, J + 1, False)
                        load(w_in, 2 * D + JW * i, J + 2, False)
                        load(w_in, 3 * D + 16 + JW * i, J + 3, False)

                if kind == "sw":
                    load(w_in, D, JOB0[l], False)
                iteration(0)
                with sp.Fori(1, ITERS) as i:
                    iteration(i)
                for n_out in range(OUT_JOBS):
                    load(w_out, JW * n_out, OUT0[l] + n_out, False)
                    if l == NL - 1 and n_out == 1:
                        sp.dma_start(shared[:],
                                     final_g.rearrange("(a n) -> a n", a=1).to_broadcast([P, D])).then_inc(final_in, 16)
            for t in range(T):
                rows_t = slice(P * t, P * t + P)
                sp.wait_ge(y_ready, 3 * t + 1)
                sp.dma_start(out[0, rows_t, 3 * JW:], qs[:, t, :]).then_inc(stored, 16)
                sp.wait_ge(y_act, t + 1)
                sp.dma_start(out[0, rows_t, 2 * JW:3 * JW], xres[:, t, 2 * JW:3 * JW]).then_inc(stored, 16)
                sp.wait_ge(y_ready, 3 * t + 3)
                sp.dma_start(out[0, rows_t, 0:2 * JW], xres[:, t, 0:2 * JW]).then_inc(stored, 16)
            sp.wait_ge(stored, 16 * 3 * T)

        @block.gpsimd
        def _(pool):
            own = Own(pool, pool_own)

            def select(ap, compare, fill, base, step, channel):
                pool.affine_select(out=ap, in_=ap, compare_op=compare, fill=fill, base=base,
                                   pattern=[[step, P]], channel_multiplier=channel).then_inc(consts, 1)

            own.step(pool.memset(ident[:], 0.0))
            own.wait()
            select(ident[:], ALU.not_equal, 1.0, 0, -1, 1)
            pool.dma_start(wg_raw[:], ml_w_in[0, :, 3 * D:3 * D + 16].rearrange("(k p) n -> p k n", p=P)).then_inc(wg_in, 16)
            for t in (masks, mask_ml):
                own.step(pool.memset(t[:], 0.0))
            for t in (ones, tri):
                own.step(pool.memset(t[:], 1.0))
            own.step(pool.memset(half_pow[:], -0.5))
            own.step(pool.memset(eps_t[:], EPS))
            for width, t in inv_width.items():
                own.step(pool.memset(t[:], 1.0 / width))
            own.wait()

            for c in (1, 3):
                select(masks[:, P * c:P * c + P], ALU.is_ge, NEG, 0, -1, 1)
            select(masks[:, 2 * P:3 * P], ALU.is_gt, NEG, 0, 1, -1)
            select(mask_ml[:], ALU.is_ge, -NEG, 0, 1, -1)
            select(tri[:], ALU.is_ge, 0.0, 0, 1, -1)

            def inverse_root(to, ms, ss, width):
                n = ms.shape[1]
                own.step(pool.tensor_tensor(ms, ss, inv_width[width][:, 0:n], ALU.mult))
                own.wait()
                own.step(pool.tensor_tensor(ms, ms, eps_t[:, 0:n], ALU.add))
                own.wait()
                return pool.tensor_tensor(to, ms, half_pow[:, 0:n], ALU.pow)

            for l in range(NL):
                pool.wait_ge(x_summed, l + 1)
                inverse_root(rstd[:], x_ms[:], x_sum[:], D).then_inc(rstd_ready, 1)
                pool.wait_ge(rstd_ready, 2 * l + 1)
                pool.tensor_scalar(rstd_half[:], rstd[:], 0.5, 0.0, ALU.mult, ALU.add).then_inc(rstd_ready, 1)
                if LAYERS[l][0] == "sw":
                    continue
                kind = LAYERS[l][0]
                with pool.Fori(0, ITERS) as i:
                    own.more = i * OWN_STEPS["pool", kind]
                    if kind == "da":
                        for h in range(2):
                            pool.wait_ge(sig["ssq_done"], in_iter(l, "ssq_done", i, 2 * h + 2))
                            inverse_root(o_rs[:, h, :], o_ms[:, h, :], o_ss[:, h, :], S).then_inc(sig["o_rstd"], 1)
                    else:
                        flat = [a[:].rearrange("p a b -> p (a b)") for a in (o_rs, o_ms, o_ss)]
                        pool.wait_ge(sig["ssq_done"], in_iter(l, "ssq_done", i, 4))
                        inverse_root(*flat, S).then_inc(sig["o_rstd"], 1)
                own.more = 0
                own.n += (ITERS - 1) * OWN_STEPS["pool", kind]
            for t in range(T):
                pool.wait_ge(x_summed, NL + t + 1)
                inverse_root(rstd[:, t:t + 1], x_ms[:, t:t + 1], x_sum[:, t:t + 1], D).then_inc(rstd_ready, 1)

        @block.scalar
        def _(act):
            def tables_of_angles():
                act.wait_ge(angles, 1)
                for n, (a, b) in enumerate(((cos_a[:], cos_b[:]), (sin_a[:, :, 1, :], sin_b[:, :, 1, :]))):
                    act.activation(a, red[:, n, :, 0:64], ACT.Sin).then_inc(tables, 1)
                    act.activation(b, red[:, n, :, 64:96], ACT.Sin).then_inc(tables, 1)

            def start_up(idx):
                if idx in (1, 3, 5):
                    x_turned_hi(-1, idx // 2 + 1)
                if idx in (2, 4, 6, 8):
                    x_squares(-1, idx // 2 - 1)
                if idx == 9:
                    tables_of_angles()
                if idx == 13:
                    act.wait_ge(angles, 2)
                    act.activation(lam_s[:], lam_s[:], ACT.Exp).then_inc(tables, 1)
                if idx == 15:
                    act.wait_ge(wg_in, 16)
                    act.activation(wg_hi[:], wg_raw[:], ACT.Copy).then_inc(tables, 1)

            def turned_hi(dst, b, name, index, cols, t_hi_at):
                act.wait_ge(full[name], index + 1)
                for c2 in range(2):
                    src = tp[b][:, S * c2:S * c2 + S]
                    col = cols[c2]
                    act.activation(dst(2 * b + c2), src, ACT.Copy, scale=1.0 if col is None else col)\
                       .then_inc(sig["t_hi"], 1)

            def x_square(l, n, t):
                if l >= 0 or n or t:
                    act.wait_ge(sig["x_sq"], in_out(l, "x_sq", 2 * n + t))
                else:
                    act.wait_ge(act_started, 1)
                act.activation(junk_x[:], xres[:, t, JW * n:JW * n + JW], ACT.Square,
                               accum_out=x_ss[:, t, n:n + 1]).then_inc(sig["x_sq"], 1)

            def x_squares(l, n):
                for t in range(T):
                    x_square(l, n, t)

            def x_turned_hi(l, n):
                if l == NL - 1:
                    return
                for b in range(2):
                    cols = [gcol[:, KC * (l + 1) + 4 * n + 2 * b + c2:KC * (l + 1) + 4 * n + 2 * b + c2 + 1] for c2 in range(2)]
                    turned_hi(lambda c: xt_hi[:, 4 * n + c, :], b, f"tp_{b}", in_out(l, f"tp_{b}", n), cols, None)

            act.wait_ge(consts, 1)
            act.activation(junk_x[:, 0:1], ident[:, 0:1], ACT.Copy).then_inc(act_started, 1)
            act.wait_ge(free["tp_0"], 1)
            x_turned_hi(-1, 0)

            def evac(l, J, i, b, dst):
                act.wait_ge(pairs_done, PAIRS * (J + 1))
                act.wait_ge(rstd_ready, 2 * l + 2)
                for t in range(T):
                    act.activation(dst[:, t, :], acc[b][t][:], ACT.Copy, scale=rstd[:, t:t + 1]).then_inc(act_emptied, 1)

            def tanh_half(l, J, i, b, dst, at):
                act.wait_ge(pairs_done, PAIRS * (J + 1))
                for t in range(T):
                    act.activation(dst[:, t, :], acc[b][t][:], ACT.Tanh, scale=rstd_half[:, t:t + 1])\
                       .then_inc(sig["tanh_done"], 1)

            def take(dst, name, b_ap, index):
                act.wait_ge(full[name], index + 1)
                act.activation(dst, b_ap, ACT.Copy).then_inc(free[name], 1)

            def exps(l, i, m, slot):
                scale = (128 if LAYERS[l][0] == "da" else 64) ** -0.5
                act.wait_ge(sig["neg_max"], in_iter(l, "neg_max", i, m + 1))
                for t in range(T):
                    cols = slice(0, P) if t == 0 else slice(P, BLK)
                    act.activation(scr[:, slot, cols], scr[:, slot, cols], ACT.Exp, bias=neg_max_t[:, slot, t:t + 1],
                                   scale=scale, accum_out=exp_sum[:, slot, t:t + 1]).then_inc(sig["exp_done"], 1)

            def squares(l, i, h, scale=None):
                act.wait_ge(full[f"sc_{h}"], in_iter(l, f"sc_{h}", i, {"da": 3, "ml": 2}[LAYERS[l][0]]))
                for t in range(T):
                    value = in_iter(l, "ssq_done", i, 2 * h + t)
                    if not (l == 0 and isinstance(i, int) and i == 0 and h + t == 0):
                        act.wait_ge(sig["ssq_done"], value)
                    act.activation(junk_o[:], sc[h][:, S * t:S * t + S], ACT.Square,
                                   scale=1.0 if scale is None else scale(h, t),
                                   accum_out=o_ss[:, h, t:t + 1]).then_inc(sig["ssq_done"], 1)

            def o_turned_hi(l, i, b, index):
                turned_hi(lambda c: ot_hi[:, bass.ds(4 * i + c, 1), :].rearrange("p a n -> p (a n)"), b, f"tp_{b}",
                          index, [scale_col(l, 0), scale_col(l, 1)], None)

            def side_da(w, l):
                def job(i, j):
                    return LOOP0[l] + 4 * i + j

                par = LOOP0[l] % 2
                if (i := w.due(DA["q_evac"])) is not None:
                    evac(l, job(i, 0), i, par, qs)
                if (i := w.due(DA["q_copy"])) is not None:
                    take(qT[:, 0:2, :], "tp_0", tp[0][:], in_iter(l, "tp_0", i, 0))
                if (i := w.due(DA["k_evac"])) is not None:
                    evac(l, job(i, 1), i, 1 - par, ks)
                if (i := w.due(DA["k_copy"])) is not None:
                    take(kT[:, 0:2, :], "tp_0", tp[0][:], in_iter(l, "tp_0", i, 1))
                if (i := w.due(DA["v_evac"])) is not None:
                    evac(l, job(i, 2), i, par, vs)
                for m in range(4):
                    if (i := w.due(DA["softmax"] + m)) is not None:
                        exps(l, i, m, m)
                if (i := w.due(DA["p_copy"][0])) is not None:
                    take(pT[:, 0, :], "tp_0", tp[0][:, 0:BLK], in_iter(l, "tp_0", i, 2))
                for h in range(2):
                    if (i := w.due(DA["ssq"][h])) is not None:
                        squares(l, i, h)
                if (i := w.due(DA["g_tanh"])) is not None:
                    tanh_half(l, job(i, 3), i, 1 - par, th, 0)
                if (i := w.due(DA["o_split"])) is not None:
                    for b in range(2):
                        o_turned_hi(l, i, b, in_iter(l, f"tp_{b}", i, 3))

            def side_sw(w, l):
                par = LOOP0[l] % 2
                if w.phase == "iter" and w.first and w.idx == SW["kv_evac"]:
                    evac(l, JOB0[l], 0, JOB0[l] % 2, ks)
                if (i := w.due(SW["q_evac"])) is not None:
                    evac(l, LOOP0[l] + 2 * i, i, par, qs)
                if (i := w.due(SW["k_copy"])) is not None:
                    take(kT[:, 0, :], "sc_1", sc[1][:, 0:S], in_iter(l, "sc_1", i, 0))
                if (i := w.due(SW["q_copy"])) is not None:
                    take(qT[:, 0:2, :], "tp_0", tp[0][:], in_iter(l, "tp_0", i, 0))
                for h in range(8):
                    if (i := w.due(SW["softmax"] + h)) is not None:
                        exps(l, i, h, h)
                    if h % 2 == 0 and (i := w.due(SW["p_copy"] + h)) is not None:
                        take(pT[:, 0, :], "tp_0", tp[0][:, 0:BLK], in_iter(l, "tp_0", i, 1 + h // 2))
                for g in range(2):
                    if (i := w.due(SW["sink"][g])) is not None:
                        act.wait_ge(sig["sink_arg"], in_iter(l, "sink_arg", i, g + 1))
                        part = sink_t[:, 4 * g:4 * g + 4, :]
                        act.activation(part, part, ACT.Exp).then_inc(sig["sink_exp"], 1)
                if (i := w.due(SW["g_tanh"])) is not None:
                    tanh_half(l, LOOP0[l] + 2 * i + 1, i, 1 - par, th, 0)
                for b in range(2):
                    if (i := w.due(sw_at(w, "o_split")[b])) is not None:
                        o_turned_hi(l, i, b, in_iter(l, f"tp_{b}", i, 5))

            to_view = scr_flat[:, 4 * BLK:4 * BLK + T * JW].rearrange("p (t n) -> p t n", t=T)

            def side_ml(w, l):
                def job(i, j):
                    return LOOP0[l] + 4 * i + j

                par = LOOP0[l] % 2
                if w.phase == "iter" and w.first:
                    if w.idx == 8:
                        act.wait_ge(gate_dve, 1)
                        act.activation(lf_e[:], lf_a[:], ACT.Exp).then_inc(gate_act, 1)
                        act.wait_ge(gate_dve, 2)
                        act.activation(lf_l[:], lf_u[:], ACT.Ln).then_inc(gate_act, 1)
                    if w.idx == 14:
                        act.wait_ge(full["tp_1"], in_head(l, "tp_1", 2))
                        act.activation(exp_nm[:], tp[1][:, 0:16].rearrange("p (t h) -> p t h", t=T), ACT.Exp, scale=-1.0)\
                           .then_inc(free["tp_1"], 1)
                        take(wide[:, 0:2, :], "tp_0", tp[0][:], in_head(l, "tp_0", 2))
                    if w.idx == 15:
                        take(wide[:, 2:4, :], "tp_1", tp[1][:], in_head(l, "tp_1", 2))
                    if w.idx == 16:
                        take(wide[:, 4:6, :], "tp_0", tp[0][:], in_head(l, "tp_0", 3))
                    if w.idx == 17:
                        take(wide[:, 6:8, :], "tp_1", tp[1][:], in_head(l, "tp_1", 3))
                if (i := w.due(ML["qk_evac"])) is not None:
                    evac(l, job(i, 0), i, par, qs)
                if (i := w.due(ML["qk_copy"])) is not None:
                    take(qT[:, 0:2, :], "tp_0", tp[0][:], in_iter(l, "tp_0", i, 0))
                for h in range(2):
                    if (i := w.due(ML["decay"][h])) is not None:
                        act.wait_ge(sig["decay_arg"], in_iter(l, "decay_arg", i, h + 1))
                        act.activation(scr[:, h, :], scr[:, h, :], ACT.Exp, scale=-1.0).then_inc(sig["exp_done"], 1)
                if (i := w.due(ML["v_evac"])) is not None:
                    evac(l, job(i, 1), i, 1 - par, vs)
                if (i := w.due(ML["ssq"])) is not None:
                    act.wait_ge(sig["den_inv"], in_iter(l, "den_inv", i, 1))
                    for h in range(2):
                        squares(l, i, h, scale=lambda h, t: den_i[:, h, t:t + 1])
                if (i := w.due(ML["o_tanh"])) is not None:
                    act.wait_ge(pairs_done, PAIRS * (job(i, 2) + 1))
                    for t in range(T):
                        act.activation(to_view[:, t, :], acc[par][t][:], ACT.Tanh, scale=rstd_half[:, t:t + 1])\
                           .then_inc(act_emptied, 1)
                if (i := w.due(ML["g_tanh"])) is not None:
                    tanh_half(l, job(i, 3), i, 1 - par, th, 0)
                if (i := w.due(ML["o_split"])) is not None:
                    o_turned_hi(l, i, 0, in_iter(l, "tp_0", i, 2))
                    o_turned_hi(l, i, 1, in_iter(l, "tp_1", i, 1))

            sides = {"da": side_da, "sw": side_sw, "ml": side_ml}

            def pair(w, j0, i, j, p):
                J = j0 + ITER_JOBS[w.kind] * i
                if (ln := w.x_due(3)) is not None:
                    wait_emptied(act, ln[0], OUT0[ln[0]] + ln[1])
                    x_squares(*ln)
                if (ln := w.x_due(5)) is not None:
                    x_turned_hi(*ln)
                sides[w.kind](w, w.l)
                if p % 2 == 0:
                    act.wait_ge(raw_full[p // 2], 16 * (J + 1))
                    if w.kind == "ml" and w.phase == "iter" and j == 0:
                        act.wait_ge(raw_half[p // 2], i * 16 + 16)
                if not (j0 == 0 and w.first and p < LAG):
                    act.wait_ge(pairs_done, PAIRS * J + p + 1 - LAG)
                q = 2 * (p % LAG)
                act.activation(w_hi[:, q:q + 2, :], raw[:, 2 * p:2 * p + 2, :], ACT.Copy).then_inc(hi_ready, 1)
                if w.start:
                    start_up(w.idx)

            for l in range(NL):
                walk(act, l, pair)
            act.wait_ge(y_gained, T * (OUT_JOBS - 1))
            for t in range(T):
                act.wait_ge(dve_emptied, emptied(NL - 1, NJOBS - 1)[1] - T + t + 1)
                x_square(NL - 1, OUT_JOBS - 1, t)
                act.wait_ge(rstd_ready, 2 * NL + t + 1)
                part = xres[:, t, 2 * JW:3 * JW]
                act.activation(part, part, ACT.Copy, scale=rstd[:, t:t + 1]).then_inc(y_act, 1)

        @block.tensor
        def _(pe):
            def fill_wait(name, index):
                if not isinstance(index, int) or index > 0:
                    pe.wait_ge(free[name], index)

            def turn(dst, src, last=None):
                n = src.shape[0]
                m = pe.transpose(dst, src, ident[0:n, 0:n])
                if last is not None:
                    m.then_inc(full[last], 1)

            def turn_eight(src, index):
                for b in range(2):
                    fill_wait(f"tp_{b}", index[b])
                    for c in range(2):
                        for t in range(T):
                            turn(tp[b][:, S * c + P * t:S * c + P * t + P],
                                 src(t)[:, P * (2 * b + c):P * (2 * b + c) + P],
                                 f"tp_{b}" if c + t == 2 else None)

            def x_turn(l, n):
                if l < NL - 1:
                    turn_eight(lambda t: xres[:, t, JW * n:JW * n + JW], [in_out(l, f"tp_{b}", n) for b in range(2)])

            pe.wait_ge(consts, 1)
            pe.wait_ge(gains_in, 48)
            turn(tp[0][:, 0:70], rows[0:70, :], "tp_0")
            pe.wait_ge(x_in[0], 16)
            x_turn(-1, 0)

            def three(out_ap, k_hi, k_lo, m_hi, m_lo, start, stop):
                pe.matmul(out_ap, k_hi, m_hi, start=start, stop=False)
                pe.matmul(out_ap, k_hi, m_lo, start=False, stop=False)
                return pe.matmul(out_ap, k_lo, m_hi, start=False, stop=stop)

            def mixed(l, i, h, p_of, index, index_full):
                name = f"sc_{h}"
                fill_wait(name, index)
                v = vs[:, :, S * h:S * h + S]
                pe.matmul(sc[h][:, 0:S], p_of(0), v[:, 0, :], start=True, stop=True)
                pe.matmul(sc[h][:, S:2 * S], p_of(1), v[:, 0, :], start=True, stop=False)
                pe.matmul(sc[h][:, S:2 * S], p_of(2), v[:, 1, :], start=False, stop=True).then_inc(full[name], 1)

            def side_da(w, l):
                if (i := w.due(DA["q_T"])) is not None:
                    pe.wait_ge(sig["roped"], in_iter(l, "roped", i, 2))
                    turn_eight(lambda t: qs[:, t, :], [in_iter(l, f"tp_{b}", i, 0) for b in range(2)])
                if (i := w.due(DA["k_T"])) is not None:
                    pe.wait_ge(sig["roped"], in_iter(l, "roped", i, 4))
                    turn_eight(lambda t: ks[:, t, :], [in_iter(l, f"tp_{b}", i, 1) for b in range(2)])
                for m in range(4):
                    if (i := w.due(DA["score"] + m)) is not None:
                        for b in range(2):
                            pe.wait_ge(free[f"tp_{b}"], in_iter(l, f"tp_{b}", i, 2))
                        name, s = f"sc_{m % 2}", sc[m % 2]
                        fill_wait(name, in_iter(l, name, i, m // 2))
                        pe.matmul(s[:, 0:P], qT[:, m, 0:P], kT[:, m, 0:P], start=True, stop=True)
                        pe.matmul(s[:, P:BLK], qT[:, m, P:S], kT[:, m, :], start=True, stop=True).then_inc(full[name], 1)
                for h in range(2):
                    if (i := w.due(DA["p_T"][h])) is not None:
                        pe.wait_ge(sig["diff_done"], in_iter(l, "diff_done", i, 2 * h + 2))
                        fill_wait(f"tp_{h}", in_iter(l, f"tp_{h}", i, 2))
                        for c in range(3):
                            turn(tp[h][:, P * c:P * c + P], scr[:, 2 * h, P * c:P * c + P], f"tp_{h}" if c == 2 else None)
                    if (i := w.due(DA["pv"][h])) is not None:
                        pe.wait_ge(free[f"tp_{h}"], in_iter(l, f"tp_{h}", i, 3))
                        wait_emptied(pe, l, LOOP0[l] + 2, i)
                        mixed(l, i, h, lambda c: pT[:, h, P * c:P * c + P], in_iter(l, f"sc_{h}", i, 2), None)
                if (i := w.due(DA["o_T"])) is not None:
                    for b in range(2):
                        pe.wait_ge(free[f"sc_{b}"], in_iter(l, f"sc_{b}", i, 3))
                    turn_eight(lambda t: gs[:, t, :], [in_iter(l, f"tp_{b}", i, 3) for b in range(2)])

            def side_sw(w, l):
                if (i := w.due(SW["k_T"])) is not None:
                    pe.wait_ge(sig["k_staged"], in_iter(l, "k_staged", i, 1))
                    fill_wait("sc_1", in_iter(l, "sc_1", i, 0))
                    for t in range(T):
                        turn(sc[1][:, P * t:P * t + P], k_stage[:, t, :, :].rearrange("p a n -> p (a n)"),
                             "sc_1" if t == 1 else None)
                if (i := w.due(SW["q_T"])) is not None:
                    pe.wait_ge(sig["roped"], in_iter(l, "roped", i, 2))
                    turn_eight(lambda t: qs[:, t, :], [in_iter(l, f"tp_{b}", i, 0) for b in range(2)])
                for h in range(8):
                    if (i := w.due(SW["pv"] + h if h < 7 else sw_at(w, "pv7"))) is not None:
                        b, g = h % 2, h // 4
                        pe.wait_ge(free[f"tp_{b}"], in_iter(l, f"tp_{b}", i, 2 + h // 2))
                        pe.wait_ge(sig["v_staged"], in_iter(l, "v_staged", i, 1))
                        if h % 4 == 0:
                            fill_wait("sc_1", in_iter(l, "sc_1", i, 1 + g))
                        o0, o1 = (sc[1][:, S * t + 64 * (h % 4):S * t + 64 * (h % 4) + 64] for t in range(T))
                        pe.matmul(o0, pT[:, b, 0:P], v_stage[:, 0, :], start=True, stop=True)
                        pe.matmul(o1, pT[:, b, P:2 * P], v_stage[:, 0, :], start=True, stop=False)
                        m = pe.matmul(o1, pT[:, b, 2 * P:BLK], v_stage[:, 1, :], start=False, stop=True)
                        if h % 4 == 3:
                            m.then_inc(full["sc_1"], 1)
                for h in range(8):
                    if (i := w.due(SW["score"] + h)) is not None:
                        if h == 0:
                            for b in range(2):
                                pe.wait_ge(free[f"tp_{b}"], in_iter(l, f"tp_{b}", i, 1))
                            pe.wait_ge(free["sc_1"], in_iter(l, "sc_1", i, 1))
                        fill_wait("sc_0", in_iter(l, "sc_0", i, h))
                        part = slice(64 * (h % 2), 64 * (h % 2) + 64)
                        q, k = qT[part, h // 2, :], kT[part, 0, :]
                        pe.matmul(sc[0][:, 0:P], q[:, 0:P], k[:, 0:P], start=True, stop=True)
                        pe.matmul(sc[0][:, P:BLK], q[:, P:S], k[:, :], start=True, stop=True).then_inc(full["sc_0"], 1)
                for h in range(8):
                    if (i := w.due(SW["p_T"] + h)) is not None:
                        b = h % 2
                        pe.wait_ge(sig["exp_done"], in_iter(l, "exp_done", i, 2 * h + 2))
                        fill_wait(f"tp_{b}", in_iter(l, f"tp_{b}", i, 1 + h // 2))
                        for c in range(3):
                            turn(tp[b][:, P * c:P * c + P], scr[:, h, P * c:P * c + P], f"tp_{b}" if c == 2 else None)
                for b in range(2):
                    if (i := w.due(sw_at(w, "o_T")[b])) is not None:
                        pe.wait_ge(free["sc_1"], in_iter(l, "sc_1", i, 2 + b))
                        fill_wait(f"tp_{b}", in_iter(l, f"tp_{b}", i, 5))
                        for c in range(2):
                            for t in range(T):
                                turn(tp[b][:, S * c + P * t:S * c + P * t + P],
                                     gs[:, t, P * (2 * b + c):P * (2 * b + c) + P], f"tp_{b}" if c + t == 2 else None)

            def gates(w, l):
                if w.idx == 3:
                    for b in range(2):
                        pe.wait_ge(free[f"tp_{b}"], in_head(l, f"tp_{b}", 0))
                    for t in range(T):
                        for k in range(KC):
                            x_k = slice(P * t, P * t + P)
                            m = three(tp[0][:, 16 * t:16 * t + 16], xt_hi[:, k, x_k], xt_lo[:, k, x_k],
                                      wg_hi[:, k, :], wg_lo[:, k, :], k == 0, k == KC - 1)
                    m.then_inc(full["tp_0"], 1)
                if w.idx == 6:
                    pe.wait_ge(gate_dve, 3)
                    pe.matmul(tp[1][:, 0:8], tri[:], lf[:, 0, :], start=True, stop=True)
                    pe.matmul(tp[1][:, 8:16], tri[:], lf[:, 1, :], start=True, stop=True)
                    pe.matmul(tp[1][:, 16:24], ones[:], lf[:, 0, :], start=True, stop=True).then_inc(full["tp_1"], 1)
                if w.idx == 8:
                    pe.wait_ge(gate_dve, 4)
                    fill_wait("tp_0", in_head(l, "tp_0", 1))
                    for n, src in enumerate((rcol[:, 0, :], rcol[:, 2, :], F_t[:, 0, :], F_t[:, 1, :])):
                        turn(tp[0][0:8, P * n:P * n + P], src, "tp_0" if n == 3 else None)
                if w.idx == 10:
                    pe.wait_ge(gate_dve, 5)
                    fill_wait("tp_1", in_head(l, "tp_1", 1))
                    for t in range(T):
                        turn(tp[1][:, 8 * t:8 * t + 8], m_r[:, t, :], "tp_1" if t == 1 else None)
                for n in range(4):
                    if w.idx == 10 + n:
                        b = n % 2
                        fill_wait(f"tp_{b}", in_head(l, f"tp_{b}", 2 + n // 2))
                        pe.matmul(tp[b][:], ones[0:8, :], scr_flat[0:8, 512 * n:512 * n + 512], start=True, stop=True)\
                          .then_inc(full[f"tp_{b}"], 1)

            def side_ml(w, l):
                if w.phase == "iter" and w.first:
                    gates(w, l)
                if (i := w.due(ML["qk_T"])) is not None:
                    wait_emptied(pe, l, LOOP0[l], i)
                    turn_eight(lambda t: qs[:, t, :], [in_iter(l, f"tp_{b}", i, 0) for b in range(2)])
                for h in range(2):
                    if (i := w.due(ML["score"][h])) is not None:
                        for b in range(2):
                            pe.wait_ge(free[f"tp_{b}"], in_iter(l, f"tp_{b}", i, 1))
                        fill_wait(f"sc_{h}", in_iter(l, f"sc_{h}", i, 0))
                        pe.matmul(sc[h][:, 0:S], kT[:, h, 0:P], qT[:, h, :], start=True, stop=True)
                        pe.matmul(sc[h][:, S:BLK], kT[:, h, P:S], qT[:, h, P:S], start=True, stop=True)\
                          .then_inc(full[f"sc_{h}"], 1)
                    if (i := w.due(ML["pv"][h])) is not None:
                        wait_emptied(pe, l, LOOP0[l] + 1, i)
                        pe.wait_ge(free[f"sc_{h}"], in_iter(l, f"sc_{h}", i, 1))
                        mixed(l, i, h, lambda c: scr[:, 2 + h, P * c:P * c + P], in_iter(l, f"sc_{h}", i, 1), None)
                        if h == 0:
                            fill_wait("tp_0", in_iter(l, "tp_0", i, 1))
                        a = [scr[:, 2 + h, P * c:P * c + P] for c in range(3)]
                        pe.matmul(tp[0][:, 2 * h:2 * h + 1], a[0], ones[:, 0:1], start=True, stop=True)
                        pe.matmul(tp[0][:, 2 * h + 1:2 * h + 2], a[1], ones[:, 0:1], start=True, stop=False)
                        m = pe.matmul(tp[0][:, 2 * h + 1:2 * h + 2], a[2], ones[:, 0:1], start=False, stop=True)
                        if h == 1:
                            m.then_inc(full["tp_0"], 1)
                if (i := w.due(ML["o_T"])) is not None:
                    for b in range(2):
                        pe.wait_ge(free[f"sc_{b}"], in_iter(l, f"sc_{b}", i, 2))
                    turn_eight(lambda t: gs[:, t, :], [in_iter(l, "tp_0", i, 2), in_iter(l, "tp_1", i, 1)])

            sides = {"da": side_da, "sw": side_sw, "ml": side_ml}

            def inputs_ready(w, j, p):
                if w.start and j == 0:
                    pe.wait_ge(free[f"tp_{p % 2}"], in_out(-1, f"tp_{p % 2}", p // 2 + 1))
                    return
                banks = {0: (0, 1), 6: (0,), 7: (1,)}.get(p, ())
                for b in banks:
                    name = f"tp_{b}"
                    if w.phase == "out" and j == 0:
                        uses = _counts(w.l, name)[1]
                        pe.wait_ge(free[name], in_iter(w.l, name, ITERS - 2 if p == 0 else ITERS - 1, uses))
                    if w.first_job_of_layer:
                        pe.wait_ge(free[name], in_out(w.l - 1, name, 3 if p == 0 else 4))

            def pair(w, j0, i, j, p):
                J = j0 + ITER_JOBS[w.kind] * i
                b = j0 % 2
                w.first_job_of_layer = j0 == JOB0[w.l] and (w.phase == "head" or w.first)
                pe.wait_ge(lo_ready, PAIRS * J + p + 1)
                if p == 0:
                    if w.phase == "iter" and not w.first and j < 2:
                        wait_emptied(pe, w.l, j0 + ITER_JOBS[w.kind] - 2, i - 1)
                    elif j0 >= 2:
                        if w.phase == "iter" and not w.first:
                            wait_emptied(pe, w.l, j0 - 2, i)
                        else:
                            l2 = max(n for n in range(NL) if JOB0[n] <= j0 - 2)
                            in_loop = LOOP0[l2] <= j0 - 2 < OUT0[l2]
                            wait_emptied(pe, l2, j0 - 2, 0)
                inputs_ready(w, j, p)
                hi, lo = (ot_hi, ot_lo) if w.phase == "out" else (xt_hi, xt_lo)

                def chunk(k, t):
                    c = slice(P * t, P * t + P)
                    return three(acc[b][t][:], hi[:, k, c], lo[:, k, c], w_hi[:, k % RING, :], w_lo[:, k % RING, :],
                                 k == 0, k == KC - 1)

                if J0_LAST == j0 and p >= PAIRS - LAG:
                    for k in (2 * p, 2 * p + 1):
                        m = chunk(k, 0)
                    if p == PAIRS - 1:
                        m.then_inc(tiles_done, 1)
                        for k in range(KC - RING, KC):
                            m = chunk(k, 1)
                        m.then_inc(tiles_done, 1)
                    return
                for k in (2 * p, 2 * p + 1):
                    for t in range(T):
                        m = chunk(k, t)
                m.then_inc(pairs_done, 1)
                if w.start and w.idx in (0, 1, 3):
                    n = {0: 1, 1: 2, 3: 3}[w.idx]
                    pe.wait_ge(x_in[n], 16)
                    x_turn(-1, n)
                if w.start and w.idx == 28:
                    pe.wait_ge(consts, 6)
                if (ln := w.x_due(1)) is not None:
                    wait_emptied(pe, ln[0], OUT0[ln[0]] + ln[1])
                    x_turn(*ln)
                sides[w.kind](w, w.l)

            for l in range(NL):
                walk(pe, l, pair)

        @block.vector
        def _(dve):
            own = Own(dve, dve_own)

            def chain(instruction):
                own.step(instruction)
                own.wait()

            TWO_PI = 2 * math.pi
            c1 = float(np.float32(6.28125))
            c2 = math.floor((TWO_PI - c1) * 2 ** 20) / 2 ** 20
            c3 = float(np.float32(TWO_PI - c1 - c2))
            LIM = 3.1415925

            def angles_step(idx):
                if idx == 4:
                    dve.wait_ge(small_in, SMALL)
                    chain(dve.tensor_copy(pos_f[:], pos_i[:]))
                    chain(dve.tensor_tensor(ang, pos_f[:].unsqueeze(2).to_broadcast([P, T, 96]),
                                            freq[:].unsqueeze(1).to_broadcast([P, T, 96]), ALU.mult))
                if idx == 5:
                    own.step(dve.tensor_scalar(turns[:, 0], ang, 1.0 / TWO_PI, 0.25, ALU.mult, ALU.add))
                    chain(dve.tensor_scalar(turns[:, 1], ang, 1.0 / TWO_PI, None, ALU.mult))
                    chain(dve.tensor_scalar(turns_flat, turns_flat, MAGIC, None, ALU.add))
                if idx == 6:
                    chain(dve.tensor_scalar(turns_flat, turns_flat, -MAGIC, None, ALU.add))
                    own.step(dve.scalar_tensor_tensor(red[:, 0], turns[:, 0], -c1, ang, ALU.mult, ALU.add))
                    chain(dve.scalar_tensor_tensor(red[:, 1], turns[:, 1], -c1, ang, ALU.mult, ALU.add))
                if idx == 7:
                    chain(dve.scalar_tensor_tensor(red_flat, turns_flat, -c2, red_flat, ALU.mult, ALU.add))
                    chain(dve.scalar_tensor_tensor(red_flat, turns_flat, -c3, red_flat, ALU.mult, ALU.add))
                if idx == 8:
                    chain(dve.tensor_scalar(red[:, 0], red[:, 0], 0.25 * TWO_PI, None, ALU.add))
                    dve.tensor_scalar(red_flat, red_flat, LIM, -LIM, ALU.min, ALU.max).then_inc(angles, 1)

            inits = [0.8 - 0.6 * math.exp(-0.3 * l) for l, (kind, _) in enumerate(LAYERS) if kind == "da"]
            dve.wait_ge(full["tp_0"], 1)
            dve.tensor_copy(gcol[:, 0:70], tp[0][:, 0:70]).then_inc(free["tp_0"], 1)
            dve.wait_ge(free["tp_0"], 1)

            def start_up(idx):
                if idx in (1, 3, 5):
                    x_turned_lo(-1, idx // 2 + 1)
                angles_step(idx)
                if idx == 9:
                    sum_squares(-1)
                if idx == 9:
                    dve.wait_ge(consts, 6)
                    dve.wait_ge(tables, 4)
                    own.step(dve.tensor_scalar(sin_a[:, :, 0, :], sin_a[:, :, 1, :], -1.0, None, ALU.mult))
                    chain(dve.tensor_scalar(sin_b[:, :, 0, :], sin_b[:, :, 1, :], -1.0, None, ALU.mult))
                if idx == 13:
                    lam_in = scr_flat[:, 0:1024].rearrange("p (l a n) -> p l a n", l=2, a=4)
                    prod = scr_flat[:, 1024:1024 + P]
                    for j in range(2):
                        for h in range(2):
                            op = dve.tensor_tensor_reduce(prod, lam_in[:, j, 2 * h, :], lam_in[:, j, 2 * h + 1, :], 1.0, 0.0,
                                                          ALU.mult, ALU.add, lam_s[:, j, h:h + 1])
                            if j + h < 2:
                                chain(op)
                            else:
                                op.then_inc(angles, 1)
                if idx == 15:
                    for j, init in enumerate(inits):
                        cols = gcol[:, NL * KC + 2 * j:NL * KC + 2 * j + 2]
                        chain(dve.tensor_scalar(cols, cols, 1.0 - init, None, ALU.mult))
                    dve.wait_ge(tables, 5)
                    for j, init in enumerate(inits):
                        chain(dve.tensor_tensor(lam[:, j:j + 1], lam_s[:, j, 0:1], lam_s[:, j, 1:2], ALU.subtract))
                        chain(dve.tensor_scalar(lam[:, j:j + 1], lam[:, j:j + 1], init, None, ALU.add))
                if idx == 16:
                    own.step(dve.tensor_scalar(sinks[:], sinks[:], -1.0, None, ALU.mult))
                    dve.wait_ge(tables, 6)
                    chain(dve.tensor_tensor(wg_lo[:], wg_raw[:], wg_hi[:].bitcast(F32), ALU.subtract))

            def turned_lo(dst_lo, dst_hi, b, name, index, cols, hi_at):
                dve.wait_ge(full[name], index + 1)
                dve.wait_ge(sig["t_hi"], hi_at + 2)
                for c2 in range(2):
                    src = tp[b][:, S * c2:S * c2 + S]
                    col = cols[c2]
                    op = dve.scalar_tensor_tensor(dst_lo(2 * b + c2), src, 1.0 if col is None else col,
                                                  dst_hi(2 * b + c2), ALU.mult, ALU.subtract)
                    if c2 == 1:
                        op.then_inc(free[name], 1)

            def x_turned_lo(l, n):
                if l == NL - 1:
                    return
                for b in range(2):
                    at = KC * (l + 1) + 4 * n + 2 * b
                    turned_lo(lambda c: xt_lo[:, 4 * n + c, :], lambda c: xt_hi[:, 4 * n + c, :].bitcast(F32), b, f"tp_{b}",
                              in_out(l, f"tp_{b}", n), [gcol[:, at + c2:at + c2 + 1] for c2 in range(2)],
                              in_out(l, "t_hi", 4 * n + 2 * b))

            def o_turned_lo(l, i, b, index, nth):
                pick = lambda buf, c: buf[:, bass.ds(4 * i + c, 1), :].rearrange("p a n -> p (a n)")
                turned_lo(lambda c: pick(ot_lo, c), lambda c: pick(ot_hi[:].bitcast(F32), c), b, f"tp_{b}", index,
                          [scale_col(l, 0), scale_col(l, 1)], in_iter(l, "t_hi", i, 2 * nth))

            def sum_squares(l):
                dve.wait_ge(sig["x_sq"], in_out(l, "x_sq", 8))
                dve.tensor_reduce(x_sum[:], x_ss[:], AX_X, ALU.add).then_inc(x_summed, 1)

            x_turned_lo(-1, 0)

            def take(dst, name, b_ap, index):
                dve.wait_ge(full[name], index + 1)
                dve.tensor_copy(dst, b_ap).then_inc(free[name], 1)

            def rope(buf, t, heads, half, cos, sin, width, before):
                if not isinstance(before, int) or before > 0:
                    dve.wait_ge(sig["roped"], before)
                xv = buf[:, t, 0:width].rearrange("p (h a n) -> p h a n", h=heads, a=2)
                a = rope_a[:, 0:width].rearrange("p (h a n) -> p h a n", h=heads, a=2)
                b = rope_b[:, 0:width].rearrange("p (h a n) -> p h a n", h=heads, a=2)
                c = cos[:, t, :].unsqueeze(1).unsqueeze(1).to_broadcast([P, heads, 2, half])
                own.step(dve.tensor_tensor(a, xv, c, ALU.mult))
                for side in range(2):
                    s = sin[:, t, side, :].unsqueeze(1).to_broadcast([P, heads, half])
                    own.step(dve.tensor_tensor(b[:, :, side, :], xv[:, :, 1 - side, :], s, ALU.mult))
                own.wait()
                dve.tensor_tensor(buf[:, t, 0:width], rope_a[:, 0:width], rope_b[:, 0:width], ALU.add)\
                   .then_inc(sig["roped"], 1)

            def row_maxima(l, i, m, slot, bank, index, mask):
                kind = LAYERS[l][0]
                name = f"sc_{bank}"
                dve.wait_ge(full[name], index + 1)
                dve.sem_inc(scores_seen)
                s = sc[bank]
                own.step(dve.tensor_tensor_reduce(scr[:, slot, 0:P], s[:, 0:P], mask_causal, 1.0, -3e38, ALU.add,
                                                  ALU.max, row_max[:, slot, 0:1]))
                dve.tensor_tensor_reduce(scr[:, slot, P:BLK], s[:, P:BLK], mask, 1.0, -3e38, ALU.add,
                                         ALU.max, row_max[:, slot, 1:2]).then_inc(free[name], 1)
                own.wait()
                dve.wait_ge(free[name], index + 1)
                if kind == "da":
                    op = dve.tensor_scalar(neg_max_t[:, slot, :], row_max[:, slot, :], -(128 ** -0.5), None, ALU.mult)
                else:
                    op = dve.tensor_scalar(neg_max_t[:, slot, :], row_max[:, slot, :], -(64 ** -0.5),
                                           sink_cur[:, slot:slot + 1], ALU.mult, ALU.min)
                op.then_inc(sig["neg_max"], 1)

            def gate(l, J, i, b, base_ap=None):
                dve.wait_ge(pairs_done, PAIRS * (J + 1))
                for t in range(T):
                    if base_ap is None:
                        dve.wait_ge(sig["tanh_done"], in_iter(l, "tanh_done", i, t + 1))
                        own.step(dve.tensor_scalar(th[:, t, :], th[:, t, :], 1.0, 0.5, ALU.add, ALU.mult))
                    else:
                        own.step(dve.tensor_scalar(base_ap[:, t, :], base_ap[:, t, :], 1.0, 0.25, ALU.add, ALU.mult))
                        own.wait()
                        dve.wait_ge(sig["tanh_done"], in_iter(l, "tanh_done", i, t + 1))
                        own.step(dve.scalar_tensor_tensor(th[:, t, :], th[:, t, :], 1.0, base_ap[:, t, :], ALU.add, ALU.mult))
                own.wait()
                for t in range(T):
                    dve.scalar_tensor_tensor(gs[:, t, :], acc[b][t][:], rstd[:, t:t + 1], th[:, t, :], ALU.mult, ALU.mult)\
                       .then_inc(dve_emptied, 1)

            def mix(l, i, factors):
                wait_emptied(dve, l, LOOP0[l] + 3, i)
                for h in range(2):
                    for t in range(T):
                        part = gs[:, t, S * h:S * h + S]
                        op = dve.scalar_tensor_tensor(part, sc[h][:, S * t:S * t + S], factors[:, h, t:t + 1], part,
                                                      ALU.mult, ALU.mult)
                        if t == 1:
                            op.then_inc(free[f"sc_{h}"], 1)

            def side_da(w, l):
                n_da = LAYERS[l][1]
                par = LOOP0[l] % 2
                for t in range(T):
                    if (i := w.due(DA["q_evac"] + t)) is not None:
                        wait_emptied(dve, l, LOOP0[l], i)
                        rope(qs, t, 4, 64, cos_a, sin_a, JW, in_iter(l, "roped", i, t))
                    if (i := w.due(DA["k_evac"] + t)) is not None:
                        wait_emptied(dve, l, LOOP0[l] + 1, i)
                        rope(ks, t, 4, 64, cos_a, sin_a, JW, in_iter(l, "roped", i, 2 + t))
                if (i := w.due(DA["q_copy"])) is not None:
                    take(qT[:, 2:4, :], "tp_1", tp[1][:], in_iter(l, "tp_1", i, 0))
                if (i := w.due(DA["k_copy"])) is not None:
                    take(kT[:, 2:4, :], "tp_1", tp[1][:], in_iter(l, "tp_1", i, 1))
                for m in range(4):
                    if (i := w.due(DA["softmax"] + m)) is not None:
                        row_maxima(l, i, m, m, m % 2, in_iter(l, f"sc_{m % 2}", i, m // 2), mask_da)
                for h in range(2):
                    if (i := w.due(DA["diff"][h])) is not None:
                        dve.wait_ge(sig["exp_done"], in_iter(l, "exp_done", i, 4 * h + 4))
                        chain(dve.reciprocal(exp_inv[:, 2 * h:2 * h + 2, :], exp_sum[:, 2 * h:2 * h + 2, :]))
                        chain(dve.tensor_scalar(exp_inv[:, 2 * h + 1, :], exp_inv[:, 2 * h + 1, :], lam[:, n_da:n_da + 1],
                                                None, ALU.mult))
                        blocks = (slice(0, P), slice(P, BLK))
                        for t, c in enumerate(blocks):
                            e1 = scr[:, 2 * h + 1, c]
                            own.step(dve.tensor_scalar(e1, e1, exp_inv[:, 2 * h + 1, t:t + 1], None, ALU.mult))
                        own.wait()
                        for t, c in enumerate(blocks):
                            dve.scalar_tensor_tensor(scr[:, 2 * h, c], scr[:, 2 * h, c], exp_inv[:, 2 * h, t:t + 1],
                                                     scr[:, 2 * h + 1, c], ALU.mult, ALU.subtract)\
                               .then_inc(sig["diff_done"], 1)
                if (i := w.due(DA["p_copy"][1])) is not None:
                    take(pT[:, 1, :], "tp_1", tp[1][:, 0:BLK], in_iter(l, "tp_1", i, 2))
                if (i := w.due(DA["gate"])) is not None:
                    gate(l, LOOP0[l] + 4 * i + 3, i, 1 - par)
                if (i := w.due(DA["mix"])) is not None:
                    dve.wait_ge(sig["o_rstd"], in_iter(l, "o_rstd", i, 2))
                    mix(l, i, o_rs)
                if (i := w.due(DA["o_split"])) is not None:
                    for b in range(2):
                        o_turned_lo(l, i, b, in_iter(l, f"tp_{b}", i, 3), b)

            def side_sw(w, l):
                par = LOOP0[l] % 2
                for t in range(T):
                    if w.phase == "iter" and w.first and w.idx == SW["kv_evac"] + 1 + t:
                        wait_emptied(dve, l, JOB0[l])
                        rope(ks, t, 4, 32, cos_b, sin_b, S, in_head(l, "roped", t))
                    if (i := w.due(SW["q_evac"] + t)) is not None:
                        wait_emptied(dve, l, LOOP0[l], i)
                        rope(qs, t, 8, 32, cos_b, sin_b, JW, in_iter(l, "roped", i, t))
                if (i := w.due(SW["k_stage"])) is not None:
                    dve.wait_ge(sig["roped"], in_head(l, "roped", 2))
                    for a in range(2):
                        own.step(dve.tensor_copy(k_stage[:, :, a, :], ks[:, :, bass.ds(64 * i, 64)]))
                    dve.tensor_copy(sink_cur[:], sinks[:, bass.ds(8 * i, 8)]).then_inc(sig["k_staged"], 1)
                if (i := w.due(SW["v_stage"])) is not None:
                    dve.tensor_copy(v_stage[:], ks[:, :, bass.ds(64 * i + S, 64)]).then_inc(sig["v_staged"], 1)
                if (i := w.due(SW["q_copy"])) is not None:
                    take(qT[:, 2:4, :], "tp_1", tp[1][:], in_iter(l, "tp_1", i, 0))
                for h in range(8):
                    if (i := w.due(SW["softmax"] + h)) is not None:
                        if h == 0:
                            dve.wait_ge(sig["k_staged"], in_iter(l, "k_staged", i, 1))
                        row_maxima(l, i, h, h, 0, in_iter(l, "sc_0", i, h), mask_sw)
                    if h % 2 and (i := w.due(SW["p_copy"] + h)) is not None:
                        take(pT[:, 1, :], "tp_1", tp[1][:, 0:BLK], in_iter(l, "tp_1", i, 1 + h // 2))
                for g in range(2):
                    four = slice(4 * g, 4 * g + 4)
                    if (i := w.due(SW["sink"][g])) is not None:
                        dve.wait_ge(sig["neg_max"], in_iter(l, "neg_max", i, 4 * g + 4))
                        minus = sink_cur[:, four].unsqueeze(2).to_broadcast([P, 4, T])
                        dve.tensor_tensor(sink_t[:, four, :], neg_max_t[:, four, :], minus, ALU.subtract)\
                           .then_inc(sig["sink_arg"], 1)
                    if (i := w.due(SW["den"][g])) is not None:
                        dve.wait_ge(sig["sink_exp"], in_iter(l, "sink_exp", i, g + 1))
                        dve.wait_ge(sig["exp_done"], in_iter(l, "exp_done", i, 8 * g + 8))
                        chain(dve.tensor_tensor(exp_sum[:, four, :], exp_sum[:, four, :], sink_t[:, four, :], ALU.add))
                        own.step(dve.reciprocal(exp_inv[:, four, :], exp_sum[:, four, :]))
                if (i := w.due(SW["gate"])) is not None:
                    gate(l, LOOP0[l] + 2 * i + 1, i, 1 - par)
                for g in range(2):
                    if (i := w.due(sw_at(w, "mix")[g])) is not None:
                        four = slice(4 * g, 4 * g + 4)
                        wait_emptied(dve, l, LOOP0[l] + 1, i)
                        dve.wait_ge(full["sc_1"], in_iter(l, "sc_1", i, 2 + g))
                        own.wait()
                        for t in range(T):
                            o = sc[1][:, S * t:S * t + S].rearrange("p (h n) -> p h n", h=4)
                            tmp = th[:, t, S * g:S * g + S]
                            inv = exp_inv[:, four, t:t + 1].to_broadcast([P, 4, 64])
                            own.step(dve.tensor_tensor(tmp.rearrange("p (h n) -> p h n", h=4), o, inv, ALU.mult))
                        own.wait()
                        for t in range(T):
                            part = gs[:, t, S * g:S * g + S]
                            op = dve.tensor_tensor(part, part, th[:, t, S * g:S * g + S], ALU.mult)
                            if t == 1:
                                op.then_inc(free["sc_1"], 1)
                for b in range(2):
                    if (i := w.due(sw_at(w, "o_split")[b])) is not None:
                        o_turned_lo(l, i, b, in_iter(l, f"tp_{b}", i, 5), b)

            def gates(w, l):
                if w.idx == 6:
                    chain(dve.memset(vs_row[:, 0:2 * RUN], -3e38))
                if w.idx == 7:
                    dve.wait_ge(full["tp_0"], in_head(l, "tp_0", 1))
                    dve.wait_ge(rstd_ready, 2 * l + 2)
                    own.step(dve.scalar_tensor_tensor(gz[:, 0, :], tp[0][:, 0:16], rstd[:, 0:1], gbias[:], ALU.mult, ALU.add))
                    dve.scalar_tensor_tensor(gz[:, 1, :], tp[0][:, 16:32], rstd[:, 1:2], gbias[:], ALU.mult, ALU.add)\
                       .then_inc(free["tp_0"], 1)
                    own.wait()
                    dve.wait_ge(free["tp_0"], in_head(l, "tp_0", 1))
                    z = gz[:, :, 8:16]
                    dve.scalar_tensor_tensor(lf_a[:], z, -1.0, z, ALU.mult, ALU.min).then_inc(gate_dve, 1)
                if w.idx == 8:
                    dve.wait_ge(gate_act, 1)
                    dve.tensor_scalar(lf_u[:], lf_e[:], 1.0, None, ALU.add).then_inc(gate_dve, 1)
                    dve.wait_ge(gate_dve, 2)
                    chain(dve.scalar_tensor_tensor(lf[:], lf_u[:], -1.0, lf_e[:], ALU.add, ALU.subtract))
                    chain(dve.reciprocal(lf_a[:], lf_u[:]))
                    chain(dve.tensor_tensor(lf[:], lf[:], lf_a[:], ALU.mult))
                    dve.wait_ge(gate_act, 2)
                    chain(dve.tensor_tensor(lf[:], lf[:], lf_l[:], ALU.subtract))
                    dve.scalar_tensor_tensor(lf[:], gz[:, :, 8:16], 0.0, lf[:], ALU.min, ALU.add).then_inc(gate_dve, 1)
                if w.idx == 10:
                    dve.wait_ge(full["tp_1"], in_head(l, "tp_1", 1))
                    dve.tensor_copy(F_t[:].rearrange("p a b -> p (a b)"), tp[1][:, 0:24]).then_inc(free["tp_1"], 1)
                    dve.wait_ge(free["tp_1"], in_head(l, "tp_1", 1))
                    own.step(dve.tensor_tensor(rcol[:, 2, :], gz[:, 1, 0:8], F_t[:, 1, :], ALU.subtract))
                    chain(dve.tensor_tensor(rcol[:, 0, :], gz[:, 0, 0:8], F_t[:, 0, :], ALU.subtract))
                    dve.tensor_tensor(rcol[:, 1, :], rcol[:, 0, :], F_t[:, 2, :], ALU.add).then_inc(gate_dve, 1)
                if w.idx == 12:
                    dve.wait_ge(full["tp_0"], in_head(l, "tp_0", 2))
                    r = tp[0][0:8, :].rearrange("p (a t n) -> p a t n", a=2, t=T)
                    own.step(dve.tensor_copy(run_a[:, :, PAD:PAD + P], r[:, 0]))
                    dve.tensor_copy(F_r[:], r[:, 1]).then_inc(free["tp_0"], 1)
                    dve.wait_ge(free["tp_0"], in_head(l, "tp_0", 2))
                    own.wait()
                    src, dst = run_a, run_b
                    for step in (1, 2, 4, 8, 16, 32, 64):
                        chain(dve.tensor_tensor(dst[:, :, PAD:PAD + P], src[:, :, PAD:PAD + P],
                                                src[:, :, PAD - step:PAD - step + P], ALU.max))
                        src, dst = dst, src
                    chain(dve.tensor_scalar(dst[:, 0, PAD:PAD + P], src[:, 0, PAD:PAD + P], 0.0, None, ALU.max))
                    chain(dve.tensor_tensor(m_end[:], dst[:, 0, PAD + P - 1:PAD + P], F_r[:, 0, P - 1:P], ALU.add))
                    chain(dve.tensor_scalar(dst[:, 1, PAD:PAD + P], src[:, 1, PAD:PAD + P], m_end[:, 0:1], None, ALU.max))
                    own.step(dve.tensor_tensor(m_r[:], dst[:, :, PAD:PAD + P], F_r[:], ALU.add))
                    diag = scr_flat[0:8, 0:8 * S].rearrange("p (h t n) -> p h t n", h=8, t=T)
                    for t in range(T):
                        op = dve.tensor_tensor(diag[:, :, t, :],
                                               dst[:, t, PAD:PAD + P].unsqueeze(1).to_broadcast([8, 8, P]),
                                               ident[0:8, 0:8].unsqueeze(2).to_broadcast([8, 8, P]), ALU.mult)
                        if t == 0:
                            own.step(op)
                        else:
                            op.then_inc(gate_dve, 1)

            to_view = scr_flat[:, 4 * BLK:4 * BLK + T * JW].rearrange("p (t n) -> p t n", t=T)

            def side_ml(w, l):
                par = LOOP0[l] % 2
                if w.phase == "iter" and w.first:
                    gates(w, l)
                if (i := w.due(ML["qk_copy"])) is not None:
                    take(kT[:, 0:2, :], "tp_1", tp[1][:], in_iter(l, "tp_1", i, 0))
                for h in range(2):
                    if (i := w.due(ML["decay"][h])) is not None:
                        if w.first:
                            dve.wait_ge(free["tp_0"], in_head(l, "tp_0", 3))
                            dve.wait_ge(gate_dve, 4)
                        else:
                            dve.wait_ge(free["tp_1"], in_head(l, "tp_1", 4))
                        head = 2 * i + h
                        for c, (t, mask) in enumerate(((0, mask_ml), (1, None), (1, mask_ml))):
                            m_t = wide[:, bass.ds(head, 1), P * t:P * t + P].rearrange("p a n -> p (a n)")
                            r = rcol[:, c, bass.ds(head, 1)]
                            d = scr[:, h, P * c:P * c + P]
                            if mask is None:
                                op = dve.tensor_scalar(d, m_t, r, 0.0, ALU.subtract, ALU.max)
                            else:
                                op = dve.scalar_tensor_tensor(d, m_t, r, mask[:], ALU.subtract, ALU.max)
                            if c == 2:
                                op.then_inc(sig["decay_arg"], 1)
                    if (i := w.due(ML["weigh"][h])) is not None:
                        dve.wait_ge(full[f"sc_{h}"], in_iter(l, f"sc_{h}", i, 1))
                        dve.wait_ge(sig["exp_done"], in_iter(l, "exp_done", i, h + 1))
                        dve.scalar_tensor_tensor(scr[:, 2 + h, :], sc[h][:, 0:BLK], 128 ** -0.5, scr[:, h, :],
                                                 ALU.mult, ALU.mult).then_inc(free[f"sc_{h}"], 1)
                if (i := w.due(ML["den"])) is not None:
                    dve.wait_ge(full["tp_0"], in_iter(l, "tp_0", i, 2))
                    flat = [a[:].rearrange("p h t -> p (h t)") for a in (den_s, den_i)]
                    chain(dve.tensor_copy(flat[0], tp[0][:, 0:4]))
                    dve.scalar_tensor_tensor(flat[1], tp[0][:, 0:4], -1.0, flat[0], ALU.mult, ALU.max)\
                       .then_inc(free["tp_0"], 1)
                    dve.wait_ge(free["tp_0"], in_iter(l, "tp_0", i, 2))
                    e = exp_nm[:, :, bass.ds(2 * i, 2)].rearrange("p t h -> p h t")
                    chain(dve.tensor_tensor(den_s[:], den_i[:], e, ALU.max))
                    dve.reciprocal(den_i[:], den_s[:]).then_inc(sig["den_inv"], 1)
                if (i := w.due(ML["comb"])) is not None:
                    dve.wait_ge(sig["o_rstd"], in_iter(l, "o_rstd", i, 1))
                    dve.wait_ge(sig["den_inv"], in_iter(l, "den_inv", i, 1))
                    own.step(dve.tensor_tensor(comb[:], den_i[:], o_rs[:], ALU.mult))
                if (i := w.due(ML["gate"])) is not None:
                    wait_emptied(dve, l, LOOP0[l] + 2, i)
                    gate(l, LOOP0[l] + 4 * i + 3, i, 1 - par, to_view)
                if (i := w.due(ML["mix"])) is not None:
                    own.wait()
                    mix(l, i, comb)
                if (i := w.due(ML["o_split"])) is not None:
                    o_turned_lo(l, i, 0, in_iter(l, "tp_0", i, 2), 0)
                    o_turned_lo(l, i, 1, in_iter(l, "tp_1", i, 1), 1)

            sides = {"da": side_da, "sw": side_sw, "ml": side_ml}

            def final_gain(n):
                dve.wait_ge(final_in, 16)
                dve.wait_ge(sig["x_sq"], in_out(NL - 1, "x_sq", 2 * n + 2))
                for t in range(T):
                    part = xres[:, t, JW * n:JW * n + JW]
                    dve.tensor_tensor(part, part, shared[:, JW * n:JW * n + JW], ALU.mult).then_inc(y_gained, 1)

            def add_residual(l, n):
                b = (OUT0[l] + n) % 2
                dve.wait_ge(pairs_done, PAIRS * (OUT0[l] + n + 1))
                for t in range(T):
                    part = xres[:, t, JW * n:JW * n + JW]
                    dve.tensor_tensor(part, part, acc[b][t][:], ALU.add).then_inc(dve_emptied, 1)

            def pair(w, j0, i, j, p):
                J = j0 + ITER_JOBS[w.kind] * i
                if (ln := w.x_due(3)) is not None:
                    add_residual(*ln)
                if (ln := w.x_due(5)) is not None:
                    x_turned_lo(*ln)
                    if ln[1] == OUT_JOBS - 1:
                        sum_squares(ln[0])
                    if ln[0] == NL - 1:
                        final_gain(ln[1])
                sides[w.kind](w, w.l)
                dve.wait_ge(hi_ready, PAIRS * J + p + 1)
                q = 2 * (p % LAG)
                dve.tensor_tensor(w_lo[:, q:q + 2, :], raw[:, 2 * p:2 * p + 2, :], w_hi[:, q:q + 2, :].bitcast(F32),
                                  ALU.subtract).then_inc(lo_ready, 1)
                if w.start:
                    start_up(w.idx)

            for l in range(NL):
                walk(dve, l, pair, own, "dve")
            last = OUT_JOBS - 1
            dve.wait_ge(y_gained, T * last)
            for t in range(T):
                dve.wait_ge(tiles_done, t + 1)
                part = xres[:, t, JW * last:JW * last + JW]
                dve.tensor_tensor(part, part, acc[J0_LAST % 2][t][:], ALU.add).then_inc(dve_emptied, 1)
                dve.wait_ge(dve_emptied, emptied(NL - 1, NJOBS - 1)[1] - T + t + 1)
                own.step(dve.tensor_tensor(qs[:, t, :], part, shared[:, JW * last:JW * last + JW], ALU.mult))
                dve.wait_ge(sig["x_sq"], in_out(NL - 1, "x_sq", 2 * last + t + 1))
                dve.tensor_reduce(x_sum[:, t:t + 1], x_ss[:, t, :], AX_X, ALU.add).then_inc(x_summed, 1)
                own.wait()
                dve.wait_ge(rstd_ready, 2 * NL + t + 1)
                for part in (qs[:, t, :], xres[:, t, 0:JW], xres[:, t, JW:2 * JW]):
                    dve.tensor_scalar(part, part, rstd[:, t:t + 1], None, ALU.mult).then_inc(y_ready, 1)


_INS = ["x", "positions", "norm_g", "final_g", "da_w_in", "da_w_out", "da_lambda", "da_subln_g", "sw_w_in", "sw_w_out",
        "sw_sinks", "ml_w_in", "ml_b_gates", "ml_w_out", "ml_norm_g"]


def kernel(**inputs):
    import numpy as _np
    import concourse.bacc as _bacc
    from concourse import mybir as _mybir
    from concourse.bass_utils import run_bass_kernel_spmd as _run

    nc = _bacc.Bacc("TRN2", target_bir_lowering=False, num_devices=1)
    arrays, args = {}, []
    given = {name: _np.ascontiguousarray(inputs[name]) for name in _INS}
    given["freqs"] = _np.concatenate([THETA ** (-_np.arange(0, d, 2, dtype=_np.float64) / d) for d in (128, 64)]).astype(_np.float32)
    for name, a in given.items():
        arrays[f"in_{name}_dram"] = a
        args.append(nc.dram_tensor(f"in_{name}_dram", a.shape, _mybir.dt.from_np(a.dtype), kind="ExternalInput").ap())
    args.append(nc.dram_tensor("out_0_dram", (1, S, D), F32, kind="ExternalOutput").ap())
    build(nc, *args)
    r = _run(nc, [arrays], core_ids=[0])
    return r.results[0]["out_0_dram"]
```

```python
import math
from contextlib import ExitStack

import numpy as np

import concourse.bass as bass
from concourse import mybir

P = 128
F32 = mybir.dt.float32
F32R = mybir.dt.float32r
I32 = mybir.dt.int32
ALU = mybir.AluOpType
ACT = mybir.ActivationFunctionType
AX_X = mybir.AxisListType.X

D = 2048
S = 256
T = S // P
KC = D // P
JW = 512
PAIRS = KC // 2
RING = 8
LAG = 4
ITERS = 4
EPS = 1e-6
NEG = -1e30
THETA = 10000.0
MAGIC = 12582912.0

LAYERS = [("da", 0), ("sw", 0), ("ml", 0), ("da", 1)]
NL = len(LAYERS)
HEAD_JOBS = {"da": 0, "sw": 1, "ml": 0}
ITER_JOBS = {"da": 4, "sw": 2, "ml": 4}
OUT_JOBS = D // JW
BLK = 3 * P

OUT_ORDER = ([(0, p) for p in range(6)] + [(1, p) for p in range(6)] + [(0, 6), (0, 7), (1, 6), (1, 7)]
             + [(n, p) for n in (2, 3) for p in range(PAIRS)])
X_SUM, X_TURN, X_SPLIT, X_END = (18, 20, 27, 3), (16, 18, 25, 1), (20, 22, 29, 5), (14, 16, 24, 32)

DA = dict(q_evac=11, q_T=10, q_copy=14, k_evac=19, k_T=18, k_copy=22, v_evac=27,
          score=20, softmax=24, diff=(26, 28), p_T=(24, 26), p_copy=(28, 30), pv=(26, 28), ssq=(30, 32),
          g_tanh=35, gate=36, mix=37, o_T=35, o_split=39)
SW = dict(kv_evac=3, k_stage=10, v_stage=12, k_T=10, k_copy=14, q_evac=11, q_T=11, q_copy=15,
          score=12, softmax=16, p_T=14, p_copy=18, pv=16, sink=(20, 24), den=(22, 26),
          g_tanh=19, gate=20, mix=(23, 27), o_T=(21, 25), o_split=(25, 29))
ML = dict(qk_evac=11, qk_T=15, qk_copy=19, score=(17, 18), decay=(18, 19), weigh=(21, 22),
          v_evac=19, pv=(20, 21), den=25, ssq=26, comb=29, o_tanh=27,
          g_tanh=35, gate=36, mix=37, o_T=35, o_split=39)

COUNTS = {
    "tp_0":      ((0, 0, 4), (0, 4, 4), (0, 6, 4), (2, 3, 4)),
    "tp_1":      ((0, 0, 4), (0, 4, 4), (0, 6, 4), (3, 3, 4)),
    "sc_0":      ((0, 0, 0), (0, 3, 0), (0, 8, 0), (2, 2, 0)),
    "sc_1":      ((1, 0, 0), (0, 3, 0), (0, 3, 0), (2, 2, 0)),
    "t_hi":      ((0, 0, 16), (0, 4, 16), (0, 4, 16), (0, 4, 16)),
    "x_sq":      ((0, 0, 8), (0, 0, 8), (0, 0, 8), (0, 0, 8)),
    "roped":     ((0, 0, 0), (0, 4, 0), (2, 2, 0), (0, 0, 0)),
    "k_staged":  ((0, 0, 0), (0, 0, 0), (0, 1, 0), (0, 0, 0)),
    "v_staged":  ((0, 0, 0), (0, 0, 0), (0, 1, 0), (0, 0, 0)),
    "neg_max":   ((0, 0, 0), (0, 4, 0), (0, 8, 0), (0, 0, 0)),
    "decay_arg": ((0, 0, 0), (0, 0, 0), (0, 0, 0), (0, 2, 0)),
    "exp_done":  ((0, 0, 0), (0, 8, 0), (0, 16, 0), (0, 2, 0)),
    "diff_done": ((0, 0, 0), (0, 4, 0), (0, 0, 0), (0, 0, 0)),
    "sink_arg":  ((0, 0, 0), (0, 0, 0), (0, 2, 0), (0, 0, 0)),
    "sink_exp":  ((0, 0, 0), (0, 0, 0), (0, 2, 0), (0, 0, 0)),
    "den_inv":   ((0, 0, 0), (0, 0, 0), (0, 0, 0), (0, 1, 0)),
    "ssq_done":  ((0, 0, 0), (0, 4, 0), (0, 0, 0), (0, 4, 0)),
    "o_rstd":    ((0, 0, 0), (0, 2, 0), (0, 0, 0), (0, 1, 0)),
    "tanh_done": ((0, 0, 0), (0, 2, 0), (0, 2, 0), (0, 2, 0)),
}
KINDS = ("start", "da", "sw", "ml")


def _bases():
    kinds = ["start"] + [k for k, _ in LAYERS]
    out = {}
    for name, by_kind in COUNTS.items():
        at, n = {}, 0
        for l, kind in enumerate(kinds):
            at[l - 1] = n
            head, per, tail = by_kind[KINDS.index(kind)]
            n += head + per * ITERS + tail
        out[name] = at
    return out


BASE = _bases()


def _counts(l, name):
    return COUNTS[name][KINDS.index("start" if l < 0 else LAYERS[l][0])]


def in_head(l, name, n):
    return BASE[name][l] + n


def in_iter(l, name, i, n):
    head, per, _ = _counts(l, name)
    return i * per + (BASE[name][l] + head + n)


def in_out(l, name, n):
    head, per, _ = _counts(l, name)
    return BASE[name][l] + head + per * ITERS + n


def _jobs():
    first, loop, out, by = [], [], [], []
    for kind, _ in LAYERS:
        first.append(len(by))
        by += ["act"] * HEAD_JOBS[kind]
        loop.append(len(by))
        by += (["act"] * (ITER_JOBS[kind] - 1) + ["dve"]) * ITERS
        out.append(len(by))
        by += ["dve"] * OUT_JOBS
    return first, loop, out, by


JOB0, LOOP0, OUT0, EMPTIED_BY = _jobs()
NJOBS = len(EMPTIED_BY)
J0_LAST = NJOBS - 1


def emptied(l, j, i=0):
    who = EMPTIED_BY[j]
    per = ITER_JOBS[LAYERS[l][0]]
    in_loop = LOOP0[l] <= j < OUT0[l]
    step = 2 * sum(w == who for w in EMPTIED_BY[LOOP0[l]:LOOP0[l] + per]) if in_loop else 0
    return who, i * step + 2 * sum(w == who for w in EMPTIED_BY[:j + 1])


class Own:

    def __init__(self, eng, sem):
        self.eng, self.sem, self.n, self.more = eng, sem, 0, 0

    def step(self, instruction):
        instruction.then_inc(self.sem, 1)
        self.n += 1

    def wait(self):
        self.eng.wait_ge(self.sem, self.more + self.n)

    def enter(self, i, per):
        self.at, self.per = self.n, per
        self.more = (i - 1) * per

    def leave(self):
        assert self.n - self.at == self.per, (self.n - self.at, self.per)
        self.n += (ITERS - 2) * self.per
        self.more = 0


OWN_STEPS = {
    ("dve", "da"): 26, ("dve", "sw"): 26, ("dve", "ml"): 11,
    ("pool", "da"): 4, ("pool", "sw"): 0, ("pool", "ml"): 2,
}


class Place:

    def __init__(self, l, phase, i, idx):
        self.l, self.kind, self.phase, self.i, self.idx = l, LAYERS[l][0], phase, i, idx
        self.period = PAIRS * ITER_JOBS[self.kind]
        self.first = isinstance(i, int)
        self.start = l == 0 and phase == "iter" and self.first

    def due(self, when):
        if self.phase == "iter" and when == self.idx:
            return self.i
        if self.phase == "iter" and when == self.idx + self.period and not self.first:
            return self.i - 1
        if self.phase == "out" and when == self.idx + self.period:
            return ITERS - 1
        return None

    def x_due(self, places):
        if self.phase == "out":
            return (self.l, places.index(self.idx)) if self.idx in places[:-1] else None
        opening = self.phase == "head" or (self.phase == "iter" and self.first and not HEAD_JOBS[self.kind])
        return (self.l - 1, OUT_JOBS - 1) if opening and self.idx == places[-1] and self.l > 0 else None


def walk(eng, l, pair, own=None, who=None):
    kind = LAYERS[l][0]
    nj = ITER_JOBS[kind]
    for p in range(PAIRS * HEAD_JOBS[kind]):
        pair(Place(l, "head", None, p), JOB0[l], 0, 0, p)
    for j in range(nj):
        for p in range(PAIRS):
            pair(Place(l, "iter", 0, j * PAIRS + p), LOOP0[l] + j, 0, j, p)
    with eng.Fori(1, ITERS) as i:
        if own:
            own.enter(i, OWN_STEPS[who, kind])
        for j in range(nj):
            for p in range(PAIRS):
                pair(Place(l, "iter", i, j * PAIRS + p), LOOP0[l] + j, i, j, p)
        if own:
            own.leave()
    for j in range(OUT_JOBS):
        for p in range(PAIRS):
            pair(Place(l, "out", None, j * PAIRS + p), OUT0[l] + j, 0, j, p)


def build(nc, x, positions, norm_g, final_g, da_w_in, da_w_out, da_lambda, da_subln_g, sw_w_in, sw_w_out,
          sw_sinks, ml_w_in, ml_b_gates, ml_w_out, ml_norm_g, freqs, out):
    ctx = ExitStack()
    with ctx:
        def sb(name, shape, dt=F32):
            return ctx.enter_context(nc.sbuf_tensor(name, shape, dt))

        def sem(name):
            return ctx.enter_context(nc.semaphore(name))

        xres = sb("xres", [P, T, D])
        xt_hi, xt_lo = sb("xt_hi", [P, KC, S], F32R), sb("xt_lo", [P, KC, S], F32R)
        ot_hi, ot_lo = sb("ot_hi", [P, KC, S], F32R), sb("ot_lo", [P, KC, S], F32R)
        raw = sb("raw", [P, KC, JW])
        w_hi, w_lo = sb("w_hi", [P, RING, JW], F32R), sb("w_lo", [P, RING, JW], F32R)
        qs, gs = (sb(n, [P, T, JW]) for n in ("qs", "gs"))
        VW = S + 1
        v_all = sb("v_all", [P, T * 2 * VW])
        vs = v_all[:, 0:T * JW].rearrange("p (t n) -> p t n", t=T)
        v_ones = v_all[:].rearrange("p (t h n) -> p t h n", t=T, h=2)
        shared = sb("shared", [P, D])
        ks = shared[:, 0:T * JW].rearrange("p (t n) -> p t n", t=T)
        rope_a, rope_b = shared[:, 2 * JW:3 * JW], shared[:, 3 * JW:4 * JW]
        ang = shared[:, 0:T * 96].rearrange("p (t n) -> p t n", t=T)
        turns_flat, red_flat = (shared[:, 512 * n:512 * n + 2 * T * 96] for n in (1, 2))
        turns, red = (a.rearrange("p (a t n) -> p a t n", a=2, t=T) for a in (turns_flat, red_flat))
        wide = shared[:].rearrange("p (h n) -> p h n", h=8)
        th = sb("th", [P, T, JW])
        qT, kT = sb("qT", [P, 4, S]), sb("kT", [P, 4, S])
        scr = sb("scr", [P, 8, BLK])
        scr_flat = scr[:].rearrange("p a b -> p (a b)")
        pT = sb("pT", [P, 2, BLK])
        junk_o, junk_x = sb("junk_o", [P, S]), sb("junk_x", [P, JW])
        ident, ones = sb("ident", [P, P]), sb("ones", [P, P])
        tri = sb("tri", [P, P])
        masks = sb("masks", [P, 4 * P])
        mask_causal, mask_da, mask_sw = masks[:, P:2 * P], masks[:, 0:2 * P], masks[:, 2 * P:4 * P]
        mask_ml = sb("mask_ml", [P, P])
        half_pow, eps_t = sb("half_pow", [P, 4]), sb("eps_t", [P, 4])
        inv_width = {n: sb(f"inv_{n}", [P, 4]) for n in (S, D)}
        rows = sb("rows", [P, P])
        gcol = sb("gcol", [P, NL * KC + 6])
        cos_a, sin_a = sb("cos_a", [P, T, 64]), sb("sin_a", [P, T, 2, 64])
        cos_b, sin_b = sb("cos_b", [P, T, 32]), sb("sin_b", [P, T, 2, 32])
        pos_i, pos_f = sb("pos_i", [P, T], I32), sb("pos_f", [P, T])
        freq = sb("freq", [P, 96])
        lam_s, lam = sb("lam_s", [P, 2, 2]), sb("lam", [P, 2])
        sinks, sink_cur = sb("sinks", [P, 32]), sb("sink_cur", [P, 8])
        k_stage, v_stage = sb("k_stage", [P, T, 2, 64]), sb("v_stage", [P, T, 64])
        row_max, neg_max_t = sb("row_max", [P, 8, T]), sb("neg_max_t", [P, 8, T])
        exp_sum, exp_inv = sb("exp_sum", [P, 8, T]), sb("exp_inv", [P, 8, T])
        sink_t = sb("sink_t", [P, 8, T])
        x_ss, x_sum, x_ms = sb("x_ss", [P, T, 4]), sb("x_sum", [P, T]), sb("x_ms", [P, T])
        rstd, rstd_half = sb("rstd", [P, T]), sb("rstd_half", [P, T])
        o_ss, o_ms, o_rs = sb("o_ss", [P, 2, T]), sb("o_ms", [P, 2, T]), sb("o_rs", [P, 2, T])
        den_s, den_i, comb = sb("den_s", [P, 2, T]), sb("den_i", [P, 2, T]), sb("comb", [P, 2, T])
        wg_raw = sb("wg_raw", [P, KC, 16])
        wg_hi, wg_lo = sb("wg_hi", [P, KC, 16], F32R), sb("wg_lo", [P, KC, 16], F32R)
        gbias, gz = sb("gbias", [P, 16]), sb("gz", [P, T, 16])
        lf_a, lf_e, lf_u, lf_l = (sb(n, [P, T, 8]) for n in ("lf_a", "lf_e", "lf_u", "lf_l"))
        lf = sb("lf", [P, T, 8])
        F_t = sb("F_t", [P, 3, 8])
        rcol = sb("rcol", [P, 3, 8])
        PAD = 64
        vs_row, gs_row = (a[0:8].rearrange("p t n -> p (t n)") for a in (vs, gs))
        RUN = T * (PAD + P)
        run_a, run_b = (vs_row[:, RUN * n:RUN * n + RUN].rearrange("p (t n) -> p t n", t=T) for n in range(2))
        F_r, m_r = (gs_row[:, S * n:S * n + S].rearrange("p (t n) -> p t n", t=T) for n in range(2))
        gate_rows = th[0:16, 0, 0:S]
        m_end = sb("m_end", [8, 1])
        exp_nm = sb("exp_nm", [P, T, 8])

        def bank(name):
            return ctx.enter_context(nc.psum_tensor(name, [P, 512], F32))

        acc = [[bank(f"acc{b}{t}") for t in range(T)] for b in range(2)]
        tp = [bank(f"tp{b}") for b in range(2)]
        sc = [bank(f"sc{b}") for b in range(2)]

        def ml_values(h, t):
            return (sc if t == 0 else tp)[h][:, 0:VW]

        raw_full = [sem(f"raw_full{s}") for s in range(4)]
        raw_half = [sem(f"raw_half{s}") for s in range(4)]
        hi_ready, lo_ready = sem("hi_ready"), sem("lo_ready")
        pairs_done = sem("pairs_done")
        act_emptied, dve_emptied = sem("act_emptied"), sem("dve_emptied")
        full = {n: sem(n + "_full") for n in ("tp_0", "tp_1", "sc_0", "sc_1")}
        free = {n: sem(n + "_free") for n in ("tp_0", "tp_1", "sc_0", "sc_1")}
        sig = {n: sem(n) for n in COUNTS if n not in full}
        tiles_done = sem("tiles_done")
        x_summed, rstd_ready = sem("x_summed"), sem("rstd_ready")
        dve_own, act_started, pool_own = sem("dve_own"), sem("act_started"), sem("pool_own")
        scores_seen = sem("scores_seen")
        gate_dve, gate_act = sem("gate_dve"), sem("gate_act")
        x_in = [sem(f"x_in{n}") for n in range(OUT_JOBS)]
        gains_in, small_in, wg_in, final_in = sem("gains_in"), sem("small_in"), sem("wg_in"), sem("final_in")
        consts, tables, angles = sem("consts"), sem("tables"), sem("angles")
        y_gained, y_ready, y_act, stored = sem("y_gained"), sem("y_ready"), sem("y_act"), sem("stored")
        SMALL = 16 * 6

        block = ctx.enter_context(nc.Block())

        def wait_emptied(eng, l, j, i=0):
            who, value = emptied(l, j, i)
            eng.wait_ge(act_emptied if who == "act" else dve_emptied, value)

        def scale_col(l, c2):
            kind, j = LAYERS[l]
            at = NL * KC + {"da": 2 * j, "ml": 4}.get(kind, 0) + c2
            return None if kind == "sw" else gcol[:, at:at + 1]

        @block.sync
        def _(sp):
            def load_x(n):
                cols = slice(JW * n, JW * n + JW)
                sp.dma_start(xres[:, :, cols], x[0, :, cols].rearrange("(t p) n -> p t n", p=P)).then_inc(x_in[n], 16)

            load_x(0)
            sp.dma_start(rows[0:64, :], norm_g.rearrange("l (c p) -> (l c) p", p=P)).then_inc(gains_in, 16)
            sp.dma_start(rows[64:68, :], da_subln_g.rearrange("l (c p) -> (l c) p", p=P)).then_inc(gains_in, 16)
            sp.dma_start(rows[68:70, :], ml_norm_g.rearrange("l (c p) -> (l c) p", p=P)).then_inc(gains_in, 16)

            def load_small():
                def small(dst, src):
                    sp.dma_start(dst, src).then_inc(small_in, 16)

                for t in range(T):
                    small(pos_i[:, t:t + 1], positions[0, P * t:P * t + P].rearrange("(p a) -> p a", a=1))
                small(freq[:], freqs.rearrange("(a n) -> a n", a=1).to_broadcast([P, 96]))
                small(scr_flat[:, 0:1024],
                      da_lambda.rearrange("l a n -> (l a n)").rearrange("(a n) -> a n", a=1).to_broadcast([P, 1024]))
                small(sinks[:], sw_sinks.to_broadcast([P, 32]))
                small(gbias[:], ml_b_gates.to_broadcast([P, 16]))

            def load_out(w, l):
                for q in range(0, len(OUT_ORDER), 2):
                    n, p = OUT_ORDER[q]
                    s = q // 2 % 4
                    sp.wait_ge(lo_ready, PAIRS * (OUT0[l] - 1) + q + 2)
                    rows_of = w[P * 2 * p:P * 2 * p + 512, :].rearrange("(k p) n -> p k n", p=P)
                    sp.dma_start(raw[:, 4 * s:4 * s + 4, :], rows_of[:, :, JW * n:JW * n + JW]).then_inc(raw_full[s], 16)
                    if l == NL - 1 and q == 2 * PAIRS:
                        sp.dma_start(shared[:],
                                     final_g.rearrange("(a n) -> a n", a=1).to_broadcast([P, D])).then_inc(final_in, 16)

            def load(w, col, J, opening, pair_of=0):
                for s in range(4):
                    if opening and s > 0:
                        load_x(s)
                    if not opening:
                        sp.wait_ge(lo_ready, PAIRS * (J - 1) + 2 * s + 2)
                    rows_of = w[512 * s:512 * s + 512, :].rearrange("(k p) n -> p k n", p=P)
                    if pair_of:
                        half = JW // 2
                        for a, arrived in enumerate((raw_half, raw_full)):
                            sp.dma_start(raw[:, 4 * s:4 * s + 4, half * a:half * a + half],
                                         rows_of[:, :, bass.ds(col + pair_of * a, half)]).then_inc(arrived[s], 16)
                    else:
                        sp.dma_start(raw[:, 4 * s:4 * s + 4, :], rows_of[:, :, bass.ds(col, JW)])\
                          .then_inc(raw_full[s], 16)

            for l, (kind, n) in enumerate(LAYERS):
                w_in = {"da": da_w_in, "sw": sw_w_in, "ml": ml_w_in}[kind][n]
                w_out = {"da": da_w_out, "sw": sw_w_out, "ml": ml_w_out}[kind][n]

                def iteration(i):
                    J = LOOP0[l] + ITER_JOBS[kind] * i
                    opening = l == 0 and isinstance(i, int)
                    if kind == "da":
                        for j in range(4):
                            load(w_in, D * j + JW * i, J + j, opening and j == 0)
                            if opening and j == 0:
                                load_small()
                    elif kind == "sw":
                        load(w_in, JW * i, J, False)
                        load(w_in, D + JW + JW * i, J + 1, False)
                    else:
                        load(w_in, JW // 2 * i, J, False, pair_of=D // 2)
                        load(w_in, D + JW * i, J + 1, False)
                        load(w_in, 2 * D + JW * i, J + 2, False)
                        load(w_in, 3 * D + 16 + JW * i, J + 3, False)

                if kind == "sw":
                    load(w_in, D, JOB0[l], False)
                iteration(0)
                with sp.Fori(1, ITERS) as i:
                    iteration(i)
                load_out(w_out, l)
            for t in range(T):
                rows_t = slice(P * t, P * t + P)
                sp.wait_ge(y_ready, 3 * t + 1)
                sp.dma_start(out[0, rows_t, 3 * JW:], qs[:, t, :]).then_inc(stored, 16)
                sp.wait_ge(y_act, t + 1)
                sp.dma_start(out[0, rows_t, 2 * JW:3 * JW], xres[:, t, 2 * JW:3 * JW]).then_inc(stored, 16)
                sp.wait_ge(y_ready, 3 * t + 3)
                sp.dma_start(out[0, rows_t, 0:2 * JW], xres[:, t, 0:2 * JW]).then_inc(stored, 16)
            sp.wait_ge(stored, 16 * 3 * T)

        @block.gpsimd
        def _(pool):
            own = Own(pool, pool_own)

            def select(ap, compare, fill, base, step, channel):
                pool.affine_select(out=ap, in_=ap, compare_op=compare, fill=fill, base=base,
                                   pattern=[[step, P]], channel_multiplier=channel).then_inc(consts, 1)

            own.step(pool.memset(ident[:], 0.0))
            own.wait()
            select(ident[:], ALU.not_equal, 1.0, 0, -1, 1)
            pool.dma_start(wg_raw[:], ml_w_in[0, :, 3 * D:3 * D + 16].rearrange("(k p) n -> p k n", p=P)).then_inc(wg_in, 16)
            for t in (masks, mask_ml):
                own.step(pool.memset(t[:], 0.0))
            for t in (ones, tri):
                own.step(pool.memset(t[:], 1.0))
            own.step(pool.memset(half_pow[:], -0.5))
            own.step(pool.memset(eps_t[:], EPS))
            for width, t in inv_width.items():
                own.step(pool.memset(t[:], 1.0 / width))
            own.wait()

            for c in (1, 3):
                select(masks[:, P * c:P * c + P], ALU.is_ge, NEG, 0, -1, 1)
            select(masks[:, 2 * P:3 * P], ALU.is_gt, NEG, 0, 1, -1)
            select(mask_ml[:], ALU.is_ge, -NEG, 0, 1, -1)
            select(tri[:], ALU.is_ge, 0.0, 0, 1, -1)

            def inverse_root(to, ms, ss, width):
                n = ms.shape[1]
                own.step(pool.tensor_tensor(ms, ss, inv_width[width][:, 0:n], ALU.mult))
                own.wait()
                own.step(pool.tensor_tensor(ms, ms, eps_t[:, 0:n], ALU.add))
                own.wait()
                return pool.tensor_tensor(to, ms, half_pow[:, 0:n], ALU.pow)

            for l in range(NL):
                pool.wait_ge(x_summed, l + 1)
                inverse_root(rstd[:], x_ms[:], x_sum[:], D).then_inc(rstd_ready, 1)
                pool.wait_ge(rstd_ready, 2 * l + 1)
                pool.tensor_scalar(rstd_half[:], rstd[:], 0.5, 0.0, ALU.mult, ALU.add).then_inc(rstd_ready, 1)
                if LAYERS[l][0] == "sw":
                    continue
                kind = LAYERS[l][0]
                with pool.Fori(0, ITERS) as i:
                    own.more = i * OWN_STEPS["pool", kind]
                    if kind == "da":
                        for h in range(2):
                            pool.wait_ge(sig["ssq_done"], in_iter(l, "ssq_done", i, 2 * h + 2))
                            inverse_root(o_rs[:, h, :], o_ms[:, h, :], o_ss[:, h, :], S).then_inc(sig["o_rstd"], 1)
                    else:
                        flat = [a[:].rearrange("p a b -> p (a b)") for a in (o_rs, o_ms, o_ss)]
                        pool.wait_ge(sig["ssq_done"], in_iter(l, "ssq_done", i, 4))
                        inverse_root(*flat, S).then_inc(sig["o_rstd"], 1)
                own.more = 0
                own.n += (ITERS - 1) * OWN_STEPS["pool", kind]
            for t in range(T):
                pool.wait_ge(x_summed, NL + t + 1)
                inverse_root(rstd[:, t:t + 1], x_ms[:, t:t + 1], x_sum[:, t:t + 1], D).then_inc(rstd_ready, 1)

        @block.scalar
        def _(act):
            def tables_of_angles():
                act.wait_ge(angles, 1)
                for n, (a, b) in enumerate(((cos_a[:], cos_b[:]), (sin_a[:, :, 1, :], sin_b[:, :, 1, :]))):
                    act.activation(a, red[:, n, :, 0:64], ACT.Sin).then_inc(tables, 1)
                    act.activation(b, red[:, n, :, 64:96], ACT.Sin).then_inc(tables, 1)

            def start_up(idx):
                if idx in (1, 3, 5):
                    x_turned_hi(-1, idx // 2 + 1)
                if idx in (2, 4, 6, 8):
                    x_squares(-1, idx // 2 - 1)
                if idx == 9:
                    tables_of_angles()
                if idx == 13:
                    act.wait_ge(angles, 2)
                    act.activation(lam_s[:], lam_s[:], ACT.Exp).then_inc(tables, 1)
                if idx == 15:
                    act.wait_ge(wg_in, 16)
                    act.activation(wg_hi[:], wg_raw[:], ACT.Copy).then_inc(tables, 1)

            def turned_hi(dst, b, name, index, cols):
                act.wait_ge(full[name], index + 1)
                for c2 in range(2):
                    src = tp[b][:, S * c2:S * c2 + S]
                    col = cols[c2]
                    act.activation(dst(2 * b + c2), src, ACT.Copy, scale=1.0 if col is None else col)\
                       .then_inc(sig["t_hi"], 1)

            def x_square(l, n, t):
                if l >= 0 or n or t:
                    act.wait_ge(sig["x_sq"], in_out(l, "x_sq", 2 * n + t))
                else:
                    act.wait_ge(act_started, 1)
                act.activation(junk_x[:], xres[:, t, JW * n:JW * n + JW], ACT.Square,
                               accum_out=x_ss[:, t, n:n + 1]).then_inc(sig["x_sq"], 1)

            def x_squares(l, n):
                for t in range(T):
                    x_square(l, n, t)

            def x_turned_hi(l, n):
                if l == NL - 1:
                    return
                for b in range(2):
                    at = KC * (l + 1) + 4 * n + 2 * b
                    cols = [gcol[:, at + c2:at + c2 + 1] for c2 in range(2)]
                    turned_hi(lambda c: xt_hi[:, 4 * n + c, :], b, f"tp_{b}", in_out(l, f"tp_{b}", n), cols)

            act.wait_ge(consts, 1)
            act.activation(junk_x[:, 0:1], ident[:, 0:1], ACT.Copy).then_inc(act_started, 1)
            act.wait_ge(free["sc_1"], 1)
            x_turned_hi(-1, 0)

            def evac(l, J, i, b, dst, heads=None):
                act.wait_ge(pairs_done, PAIRS * (J + 1))
                act.wait_ge(rstd_ready, 2 * l + 2)
                for t in range(T):
                    src = acc[b][t][:]
                    if heads:
                        src = src.rearrange("p (h n) -> p h n", h=heads)
                    act.activation(dst[:, t], src, ACT.Copy, scale=rstd[:, t:t + 1]).then_inc(act_emptied, 1)

            def tanh_half(l, J, i, b, dst):
                act.wait_ge(pairs_done, PAIRS * (J + 1))
                for t in range(T):
                    act.activation(dst[:, t, :], acc[b][t][:], ACT.Tanh, scale=rstd_half[:, t:t + 1])\
                       .then_inc(sig["tanh_done"], 1)

            def take(dst, name, b_ap, index):
                act.wait_ge(full[name], index + 1)
                act.activation(dst, b_ap, ACT.Copy).then_inc(free[name], 1)

            def exps(l, i, m, slot):
                scale = (128 if LAYERS[l][0] == "da" else 64) ** -0.5
                act.wait_ge(sig["neg_max"], in_iter(l, "neg_max", i, m + 1))
                for t in range(T):
                    cols = slice(0, P) if t == 0 else slice(P, BLK)
                    act.activation(scr[:, slot, cols], scr[:, slot, cols], ACT.Exp, bias=neg_max_t[:, slot, t:t + 1],
                                   scale=scale, accum_out=exp_sum[:, slot, t:t + 1]).then_inc(sig["exp_done"], 1)

            def squares(l, i, h, scale=None):
                ml = LAYERS[l][0] == "ml"
                act.wait_ge(full[f"sc_{h}"], in_iter(l, f"sc_{h}", i, 2 if ml else 3))
                if ml:
                    act.wait_ge(full[f"tp_{h}"], in_iter(l, f"tp_{h}", i, 2))
                for t in range(T):
                    value = in_iter(l, "ssq_done", i, 2 * h + t)
                    if not (l == 0 and isinstance(i, int) and i == 0 and h + t == 0):
                        act.wait_ge(sig["ssq_done"], value)
                    act.activation(junk_o[:], ml_values(h, t)[:, 0:S] if ml else sc[h][:, S * t:S * t + S], ACT.Square,
                                   scale=1.0 if scale is None else scale(h, t),
                                   accum_out=o_ss[:, h, t:t + 1]).then_inc(sig["ssq_done"], 1)

            def o_turned_hi(l, i, b, index):
                turned_hi(lambda c: ot_hi[:, bass.ds(4 * i + c, 1), :].rearrange("p a n -> p (a n)"), b, f"tp_{b}",
                          index, [scale_col(l, 0), scale_col(l, 1)])

            def side_da(w, l):
                def job(i, j):
                    return LOOP0[l] + 4 * i + j

                par = LOOP0[l] % 2
                if (i := w.due(DA["q_evac"])) is not None:
                    evac(l, job(i, 0), i, par, qs)
                if (i := w.due(DA["q_copy"])) is not None:
                    take(qT[:, 0:2, :], "tp_0", tp[0][:], in_iter(l, "tp_0", i, 0))
                if (i := w.due(DA["k_evac"])) is not None:
                    evac(l, job(i, 1), i, 1 - par, ks)
                if (i := w.due(DA["k_copy"])) is not None:
                    take(kT[:, 0:2, :], "tp_0", tp[0][:], in_iter(l, "tp_0", i, 1))
                if (i := w.due(DA["v_evac"])) is not None:
                    evac(l, job(i, 2), i, par, vs)
                for m in range(4):
                    if (i := w.due(DA["softmax"] + m)) is not None:
                        exps(l, i, m, m)
                if (i := w.due(DA["p_copy"][0])) is not None:
                    take(pT[:, 0, :], "tp_0", tp[0][:, 0:BLK], in_iter(l, "tp_0", i, 2))
                for h in range(2):
                    if (i := w.due(DA["ssq"][h])) is not None:
                        squares(l, i, h)
                if (i := w.due(DA["g_tanh"])) is not None:
                    tanh_half(l, job(i, 3), i, 1 - par, th)
                if (i := w.due(DA["o_split"])) is not None:
                    for b in range(2):
                        o_turned_hi(l, i, b, in_iter(l, f"tp_{b}", i, 3))

            def side_sw(w, l):
                par = LOOP0[l] % 2
                if w.phase == "iter" and w.first and w.idx == SW["kv_evac"]:
                    evac(l, JOB0[l], 0, JOB0[l] % 2, ks)
                if (i := w.due(SW["q_evac"])) is not None:
                    evac(l, LOOP0[l] + 2 * i, i, par, qs)
                if (i := w.due(SW["k_copy"])) is not None:
                    take(kT[:, 0, :], "sc_1", sc[1][:, 0:S], in_iter(l, "sc_1", i, 0))
                if (i := w.due(SW["q_copy"])) is not None:
                    take(qT[:, 0:2, :], "tp_0", tp[0][:], in_iter(l, "tp_0", i, 0))
                for h in range(8):
                    if (i := w.due(SW["softmax"] + h)) is not None:
                        exps(l, i, h, h)
                    if h % 2 == 0 and (i := w.due(SW["p_copy"] + h)) is not None:
                        take(pT[:, 0, :], "tp_0", tp[0][:, 0:BLK], in_iter(l, "tp_0", i, 1 + h // 2))
                for g in range(2):
                    if (i := w.due(SW["sink"][g])) is not None:
                        act.wait_ge(sig["sink_arg"], in_iter(l, "sink_arg", i, g + 1))
                        part = sink_t[:, 4 * g:4 * g + 4, :]
                        act.activation(part, part, ACT.Exp).then_inc(sig["sink_exp"], 1)
                if (i := w.due(SW["g_tanh"])) is not None:
                    tanh_half(l, LOOP0[l] + 2 * i + 1, i, 1 - par, th)

            def side_sw_first(w, l):
                for b in range(2):
                    if (i := w.due(SW["o_split"][b])) is not None:
                        o_turned_hi(l, i, b, in_iter(l, f"tp_{b}", i, 5))

            to_view = scr_flat[:, 4 * BLK:4 * BLK + T * JW].rearrange("p (t n) -> p t n", t=T)

            def side_ml(w, l):
                def job(i, j):
                    return LOOP0[l] + 4 * i + j

                par = LOOP0[l] % 2
                if w.phase == "iter" and w.first:
                    if w.idx == 10:
                        act.wait_ge(gate_dve, 1)
                        act.activation(lf_e[:], lf_a[:], ACT.Exp).then_inc(gate_act, 1)
                        act.wait_ge(gate_dve, 2)
                        act.activation(lf_l[:], lf_u[:], ACT.Ln).then_inc(gate_act, 1)
                    if w.idx == 17:
                        act.wait_ge(full["tp_1"], in_head(l, "tp_1", 3))
                        act.activation(exp_nm[:], tp[1][:, 0:16].rearrange("p (t h) -> p t h", t=T), ACT.Exp, scale=-1.0)\
                           .then_inc(free["tp_1"], 1)
                    for n in range(4):
                        if w.idx == 17 + min(n, 2):
                            name = f"sc_{n % 2}"
                            take(wide[:, 2 * n:2 * n + 2, :], name, sc[n % 2][:], in_head(l, name, n // 2))
                if (i := w.due(ML["qk_evac"])) is not None:
                    evac(l, job(i, 0), i, par, qs)
                if (i := w.due(ML["qk_copy"])) is not None:
                    take(qT[:, 0:2, :], "tp_0", tp[0][:], in_iter(l, "tp_0", i, 0))
                for h in range(2):
                    if (i := w.due(ML["decay"][h])) is not None:
                        act.wait_ge(sig["decay_arg"], in_iter(l, "decay_arg", i, h + 1))
                        act.activation(scr[:, h, :], scr[:, h, :], ACT.Exp, scale=-1.0).then_inc(sig["exp_done"], 1)
                if (i := w.due(ML["v_evac"])) is not None:
                    evac(l, job(i, 1), i, 1 - par, v_ones[:, :, :, 0:S], heads=2)
                if (i := w.due(ML["ssq"])) is not None:
                    act.wait_ge(sig["den_inv"], in_iter(l, "den_inv", i, 1))
                    for h in range(2):
                        squares(l, i, h, scale=lambda h, t: den_i[:, h, t:t + 1])
                if (i := w.due(ML["o_tanh"])) is not None:
                    act.wait_ge(pairs_done, PAIRS * (job(i, 2) + 1))
                    for t in range(T):
                        act.activation(to_view[:, t, :], acc[par][t][:], ACT.Tanh, scale=rstd_half[:, t:t + 1])\
                           .then_inc(act_emptied, 1)
                if (i := w.due(ML["g_tanh"])) is not None:
                    tanh_half(l, job(i, 3), i, 1 - par, th)
                if (i := w.due(ML["o_split"])) is not None:
                    o_turned_hi(l, i, 0, in_iter(l, "tp_0", i, 2))
                    o_turned_hi(l, i, 1, in_iter(l, "tp_1", i, 2))

            sides = {"da": side_da, "sw": side_sw, "ml": side_ml}

            def pair(w, j0, i, j, p):
                J = j0 + ITER_JOBS[w.kind] * i
                if (ln := w.x_due(X_SUM)) is not None:
                    wait_emptied(act, ln[0], OUT0[ln[0]] + ln[1])
                    x_squares(*ln)
                if (ln := w.x_due(X_SPLIT)) is not None:
                    x_turned_hi(*ln)
                if w.kind == "sw":
                    side_sw_first(w, w.l)
                else:
                    sides[w.kind](w, w.l)
                if p % 2 == 0:
                    act.wait_ge(raw_full[p // 2], 16 * (J + 1))
                    if w.kind == "ml" and w.phase == "iter" and j == 0:
                        act.wait_ge(raw_half[p // 2], i * 16 + 16)
                if not (j0 == 0 and w.first and p < LAG):
                    act.wait_ge(pairs_done, PAIRS * J + p + 1 - LAG)
                q = 2 * (p % LAG)
                act.activation(w_hi[:, q:q + 2, :], raw[:, 2 * p:2 * p + 2, :], ACT.Copy).then_inc(hi_ready, 1)
                if w.kind == "sw":
                    sides[w.kind](w, w.l)
                if w.start:
                    start_up(w.idx)

            for l in range(NL):
                walk(act, l, pair)
            act.wait_ge(y_gained, T * (OUT_JOBS - 1))
            for t in range(T):
                act.wait_ge(dve_emptied, emptied(NL - 1, NJOBS - 1)[1] - T + t + 1)
                x_square(NL - 1, OUT_JOBS - 1, t)
                act.wait_ge(rstd_ready, 2 * NL + t + 1)
                part = xres[:, t, 2 * JW:3 * JW]
                act.activation(part, part, ACT.Copy, scale=rstd[:, t:t + 1]).then_inc(y_act, 1)

        @block.tensor
        def _(pe):
            def fill_wait(name, index):
                if not isinstance(index, int) or index > 0:
                    pe.wait_ge(free[name], index)

            def turn(dst, src, last=None):
                n = src.shape[0]
                m = pe.transpose(dst, src, ident[0:n, 0:n])
                if last is not None:
                    m.then_inc(full[last], 1)

            def turn_eight(src, index):
                for b in range(2):
                    fill_wait(f"tp_{b}", index[b])
                    for c in range(2):
                        for t in range(T):
                            turn(tp[b][:, S * c + P * t:S * c + P * t + P],
                                 src(t)[:, P * (2 * b + c):P * (2 * b + c) + P],
                                 f"tp_{b}" if c + t == 2 else None)

            def x_turn(l, n):
                if l < NL - 1:
                    turn_eight(lambda t: xres[:, t, JW * n:JW * n + JW], [in_out(l, f"tp_{b}", n) for b in range(2)])

            pe.wait_ge(consts, 1)
            pe.wait_ge(x_in[0], 16)
            x_turn(-1, 0)
            pe.wait_ge(gains_in, 48)
            turn(sc[1][:, 0:70], rows[0:70, :], "sc_1")
            for _ in range(10):
                pe.matmul(sc[0][:, 0:P], ident[:], ident[:], start=True, stop=True)

            def three(out_ap, k_hi, k_lo, m_hi, m_lo, start, stop):
                pe.matmul(out_ap, k_hi, m_hi, start=start, stop=False)
                pe.matmul(out_ap, k_hi, m_lo, start=False, stop=False)
                return pe.matmul(out_ap, k_lo, m_hi, start=False, stop=stop)

            def mixed(h, p_of, index):
                name = f"sc_{h}"
                fill_wait(name, index)
                v = vs[:, :, S * h:S * h + S]
                pe.matmul(sc[h][:, 0:S], p_of(0), v[:, 0, :], start=True, stop=True)
                pe.matmul(sc[h][:, S:2 * S], p_of(1), v[:, 0, :], start=True, stop=False)
                pe.matmul(sc[h][:, S:2 * S], p_of(2), v[:, 1, :], start=False, stop=True).then_inc(full[name], 1)

            def side_da(w, l):
                if (i := w.due(DA["q_T"])) is not None:
                    pe.wait_ge(sig["roped"], in_iter(l, "roped", i, 2))
                    turn_eight(lambda t: qs[:, t, :], [in_iter(l, f"tp_{b}", i, 0) for b in range(2)])
                if (i := w.due(DA["k_T"])) is not None:
                    pe.wait_ge(sig["roped"], in_iter(l, "roped", i, 4))
                    turn_eight(lambda t: ks[:, t, :], [in_iter(l, f"tp_{b}", i, 1) for b in range(2)])
                for m in range(4):
                    if (i := w.due(DA["score"] + m)) is not None:
                        for b in range(2):
                            pe.wait_ge(free[f"tp_{b}"], in_iter(l, f"tp_{b}", i, 2))
                        name, s = f"sc_{m % 2}", sc[m % 2]
                        fill_wait(name, in_iter(l, name, i, m // 2))
                        pe.matmul(s[:, 0:P], qT[:, m, 0:P], kT[:, m, 0:P], start=True, stop=True)
                        pe.matmul(s[:, P:BLK], qT[:, m, P:S], kT[:, m, :], start=True, stop=True).then_inc(full[name], 1)
                for h in range(2):
                    if (i := w.due(DA["p_T"][h])) is not None:
                        pe.wait_ge(sig["diff_done"], in_iter(l, "diff_done", i, 2 * h + 2))
                        fill_wait(f"tp_{h}", in_iter(l, f"tp_{h}", i, 2))
                        for c in range(3):
                            turn(tp[h][:, P * c:P * c + P], scr[:, 2 * h, P * c:P * c + P], f"tp_{h}" if c == 2 else None)
                    if (i := w.due(DA["pv"][h])) is not None:
                        pe.wait_ge(free[f"tp_{h}"], in_iter(l, f"tp_{h}", i, 3))
                        wait_emptied(pe, l, LOOP0[l] + 2, i)
                        mixed(h, lambda c: pT[:, h, P * c:P * c + P], in_iter(l, f"sc_{h}", i, 2))
                if (i := w.due(DA["o_T"])) is not None:
                    for b in range(2):
                        pe.wait_ge(free[f"sc_{b}"], in_iter(l, f"sc_{b}", i, 3))
                    turn_eight(lambda t: gs[:, t, :], [in_iter(l, f"tp_{b}", i, 3) for b in range(2)])

            def side_sw(w, l):
                if (i := w.due(SW["k_T"])) is not None:
                    pe.wait_ge(sig["k_staged"], in_iter(l, "k_staged", i, 1))
                    fill_wait("sc_1", in_iter(l, "sc_1", i, 0))
                    for t in range(T):
                        turn(sc[1][:, P * t:P * t + P], k_stage[:, t, :, :].rearrange("p a n -> p (a n)"),
                             "sc_1" if t == 1 else None)
                if (i := w.due(SW["q_T"])) is not None:
                    pe.wait_ge(sig["roped"], in_iter(l, "roped", i, 2))
                    turn_eight(lambda t: qs[:, t, :], [in_iter(l, f"tp_{b}", i, 0) for b in range(2)])
                for h in range(8):
                    if (i := w.due(SW["pv"] + h)) is not None:
                        b, g = h % 2, h // 4
                        pe.wait_ge(free[f"tp_{b}"], in_iter(l, f"tp_{b}", i, 2 + h // 2))
                        pe.wait_ge(sig["v_staged"], in_iter(l, "v_staged", i, 1))
                        if h % 4 == 0:
                            fill_wait("sc_1", in_iter(l, "sc_1", i, 1 + g))
                        o0, o1 = (sc[1][:, S * t + 64 * (h % 4):S * t + 64 * (h % 4) + 64] for t in range(T))
                        pe.matmul(o0, pT[:, b, 0:P], v_stage[:, 0, :], start=True, stop=True)
                        pe.matmul(o1, pT[:, b, P:2 * P], v_stage[:, 0, :], start=True, stop=False)
                        m = pe.matmul(o1, pT[:, b, 2 * P:BLK], v_stage[:, 1, :], start=False, stop=True)
                        if h % 4 == 3:
                            m.then_inc(full["sc_1"], 1)
                for h in range(8):
                    if (i := w.due(SW["score"] + h)) is not None:
                        if h == 0:
                            for b in range(2):
                                pe.wait_ge(free[f"tp_{b}"], in_iter(l, f"tp_{b}", i, 1))
                            pe.wait_ge(free["sc_1"], in_iter(l, "sc_1", i, 1))
                        fill_wait("sc_0", in_iter(l, "sc_0", i, h))
                        part = slice(64 * (h % 2), 64 * (h % 2) + 64)
                        q, k = qT[part, h // 2, :], kT[part, 0, :]
                        pe.matmul(sc[0][:, 0:P], q[:, 0:P], k[:, 0:P], start=True, stop=True)
                        pe.matmul(sc[0][:, P:BLK], q[:, P:S], k[:, :], start=True, stop=True).then_inc(full["sc_0"], 1)
                for h in range(8):
                    if (i := w.due(SW["p_T"] + h)) is not None:
                        b = h % 2
                        pe.wait_ge(sig["exp_done"], in_iter(l, "exp_done", i, 2 * h + 2))
                        fill_wait(f"tp_{b}", in_iter(l, f"tp_{b}", i, 1 + h // 2))
                        for c in range(3):
                            turn(tp[b][:, P * c:P * c + P], scr[:, h, P * c:P * c + P], f"tp_{b}" if c == 2 else None)
                for b in range(2):
                    if (i := w.due(SW["o_T"][b])) is not None:
                        pe.wait_ge(free["sc_1"], in_iter(l, "sc_1", i, 2 + b))
                        fill_wait(f"tp_{b}", in_iter(l, f"tp_{b}", i, 5))
                        for c in range(2):
                            for t in range(T):
                                turn(tp[b][:, S * c + P * t:S * c + P * t + P],
                                     gs[:, t, P * (2 * b + c):P * (2 * b + c) + P], f"tp_{b}" if c + t == 2 else None)

            def gates(w, l):
                if w.idx == 2:
                    for b in range(2):
                        pe.wait_ge(free[f"tp_{b}"], in_head(l, f"tp_{b}", 0))
                    for k in range(KC):
                        m = three(tp[0][0:16, 0:S], wg_hi[:, k, :], wg_lo[:, k, :], xt_hi[:, k, :], xt_lo[:, k, :],
                                  k == 0, k == KC - 1)
                    m.then_inc(full["tp_0"], 1)
                if w.idx == 4:
                    pe.wait_ge(free["tp_0"], in_head(l, "tp_0", 1))
                    for t in range(T):
                        turn(tp[1][:, 16 * t:16 * t + 16], gate_rows[:, P * t:P * t + P], "tp_1" if t == 1 else None)
                if w.idx == 7:
                    pe.wait_ge(gate_dve, 3)
                    pe.matmul(tp[1][:, 0:8], tri[:], lf[:, 0, :], start=True, stop=True)
                    pe.matmul(tp[1][:, 8:16], tri[:], lf[:, 1, :], start=True, stop=True)
                    pe.matmul(tp[1][:, 16:24], ones[:], lf[:, 0, :], start=True, stop=True).then_inc(full["tp_1"], 1)
                if w.idx == 9:
                    pe.wait_ge(gate_dve, 4)
                    for n, src in enumerate((rcol[:, 0, :], rcol[:, 2, :], F_t[:, 0, :], F_t[:, 1, :])):
                        turn(tp[0][0:8, P * n:P * n + P], src, "tp_0" if n == 3 else None)
                if w.idx == 12:
                    pe.wait_ge(gate_dve, 5)
                    for t in range(T):
                        turn(tp[1][:, 8 * t:8 * t + 8], m_r[:, t, :], "tp_1" if t == 1 else None)
                for n in range(4):
                    if w.idx == 12 + n:
                        b = n % 2
                        fill_wait(f"sc_{b}", in_head(l, f"sc_{b}", n // 2))
                        for c in range(2):
                            head = 2 * n + c
                            m = pe.matmul(sc[b][:, S * c:S * c + S], ident[0:8, head:head + 1].to_broadcast([8, P]),
                                          run_a[:, :, PAD:PAD + P], start=True, stop=True)
                        m.then_inc(full[f"sc_{b}"], 1)

            def side_ml(w, l):
                if w.phase == "iter" and w.first:
                    gates(w, l)
                if (i := w.due(ML["qk_T"])) is not None:
                    wait_emptied(pe, l, LOOP0[l], i)
                    turn_eight(lambda t: qs[:, t, :], [in_iter(l, f"tp_{b}", i, 0) for b in range(2)])
                for h in range(2):
                    if (i := w.due(ML["score"][h])) is not None:
                        for b in range(2):
                            pe.wait_ge(free[f"tp_{b}"], in_iter(l, f"tp_{b}", i, 1))
                        fill_wait(f"sc_{h}", in_iter(l, f"sc_{h}", i, 0))
                        pe.matmul(sc[h][:, 0:S], kT[:, h, 0:P], qT[:, h, :], start=True, stop=True)
                        pe.matmul(sc[h][:, S:BLK], kT[:, h, P:S], qT[:, h, P:S], start=True, stop=True)\
                          .then_inc(full[f"sc_{h}"], 1)
                    if (i := w.due(ML["pv"][h])) is not None:
                        wait_emptied(pe, l, LOOP0[l] + 1, i)
                        pe.wait_ge(free[f"sc_{h}"], in_iter(l, f"sc_{h}", i, 1))
                        pe.wait_ge(gate_dve, 6)
                        fill_wait(f"sc_{h}", in_iter(l, f"sc_{h}", i, 1))
                        fill_wait(f"tp_{h}", in_iter(l, f"tp_{h}", i, 1))
                        a = [scr[:, 2 + h, P * c:P * c + P] for c in range(3)]
                        v0, v1 = v_ones[:, 0, h, :], v_ones[:, 1, h, :]
                        pe.matmul(ml_values(h, 0), a[0], v0, start=True, stop=True).then_inc(full[f"sc_{h}"], 1)
                        pe.matmul(ml_values(h, 1), a[1], v0, start=True, stop=False)
                        pe.matmul(ml_values(h, 1), a[2], v1, start=False, stop=True).then_inc(full[f"tp_{h}"], 1)
                if (i := w.due(ML["o_T"])) is not None:
                    for b in range(2):
                        pe.wait_ge(free[f"sc_{b}"], in_iter(l, f"sc_{b}", i, 2))
                    turn_eight(lambda t: gs[:, t, :], [in_iter(l, "tp_0", i, 2), in_iter(l, "tp_1", i, 2)])

            sides = {"da": side_da, "sw": side_sw, "ml": side_ml}

            def inputs_ready(w, j, p):
                if w.start and j == 0:
                    pe.wait_ge(free[f"tp_{p % 2}"], in_out(-1, f"tp_{p % 2}", p // 2 + 1))
                    return
                for b in {0: (0, 1), 6: (0,), 7: (1,)}.get(p, ()):
                    name = f"tp_{b}"
                    if w.phase == "out" and j == 0:
                        uses = _counts(w.l, name)[1]
                        pe.wait_ge(free[name], in_iter(w.l, name, ITERS - 2 if p == 0 else ITERS - 1, uses))
                    if w.first_job_of_layer:
                        pe.wait_ge(free[name], in_out(w.l - 1, name, 3 if p == 0 else 4))

            def pair(w, j0, i, j, p):
                J = j0 + ITER_JOBS[w.kind] * i
                w.first_job_of_layer = j0 == JOB0[w.l] and (w.phase == "head" or w.first)
                pe.wait_ge(lo_ready, PAIRS * J + p + 1)
                slot = 2 * (p % LAG)
                if w.phase == "out":
                    j, p = OUT_ORDER[w.idx]
                    j0 = OUT0[w.l] + j
                b = j0 % 2
                if p == 0:
                    if w.phase == "iter" and not w.first and j < 2:
                        wait_emptied(pe, w.l, j0 + ITER_JOBS[w.kind] - 2, i - 1)
                    elif j0 >= 2:
                        if w.phase == "iter" and not w.first:
                            wait_emptied(pe, w.l, j0 - 2, i)
                        else:
                            l2 = max(n for n in range(NL) if JOB0[n] <= j0 - 2)
                            wait_emptied(pe, l2, j0 - 2, 0)
                inputs_ready(w, j, p)
                hi, lo = (ot_hi, ot_lo) if w.phase == "out" else (xt_hi, xt_lo)

                def chunk(k, t):
                    c = slice(P * t, P * t + P)
                    at = (slot + k - 2 * p) % RING
                    return three(acc[b][t][:], hi[:, k, c], lo[:, k, c], w_hi[:, at, :], w_lo[:, at, :],
                                 k == 0, k == KC - 1)

                if J0_LAST == j0 and p >= PAIRS - LAG:
                    for k in (2 * p, 2 * p + 1):
                        m = chunk(k, 0)
                    if p == PAIRS - 1:
                        m.then_inc(tiles_done, 1)
                        for k in range(KC - RING, KC):
                            m = chunk(k, 1)
                        m.then_inc(tiles_done, 1)
                    return
                for k in (2 * p, 2 * p + 1):
                    for t in range(T):
                        m = chunk(k, t)
                m.then_inc(pairs_done, 1)
                if w.start and w.idx in (0, 1, 3):
                    n = {0: 1, 1: 2, 3: 3}[w.idx]
                    pe.wait_ge(x_in[n], 16)
                    x_turn(-1, n)
                if w.start and w.idx == 28:
                    pe.wait_ge(consts, 6)
                if (ln := w.x_due(X_TURN)) is not None:
                    wait_emptied(pe, ln[0], OUT0[ln[0]] + ln[1])
                    x_turn(*ln)
                sides[w.kind](w, w.l)

            for l in range(NL):
                walk(pe, l, pair)

        @block.vector
        def _(dve):
            own = Own(dve, dve_own)

            def chain(instruction):
                own.step(instruction)
                own.wait()

            TWO_PI = 2 * math.pi
            c1 = float(np.float32(6.28125))
            c2 = math.floor((TWO_PI - c1) * 2 ** 20) / 2 ** 20
            c3 = float(np.float32(TWO_PI - c1 - c2))
            LIM = 3.1415925

            def angles_step(idx):
                if idx == 4:
                    dve.wait_ge(small_in, SMALL)
                    chain(dve.tensor_copy(pos_f[:], pos_i[:]))
                    chain(dve.tensor_tensor(ang, pos_f[:].unsqueeze(2).to_broadcast([P, T, 96]),
                                            freq[:].unsqueeze(1).to_broadcast([P, T, 96]), ALU.mult))
                if idx == 5:
                    own.step(dve.tensor_scalar(turns[:, 0], ang, 1.0 / TWO_PI, 0.25, ALU.mult, ALU.add))
                    chain(dve.tensor_scalar(turns[:, 1], ang, 1.0 / TWO_PI, None, ALU.mult))
                    chain(dve.tensor_scalar(turns_flat, turns_flat, MAGIC, None, ALU.add))
                if idx == 6:
                    chain(dve.tensor_scalar(turns_flat, turns_flat, -MAGIC, None, ALU.add))
                    own.step(dve.scalar_tensor_tensor(red[:, 0], turns[:, 0], -c1, ang, ALU.mult, ALU.add))
                    chain(dve.scalar_tensor_tensor(red[:, 1], turns[:, 1], -c1, ang, ALU.mult, ALU.add))
                if idx == 7:
                    chain(dve.scalar_tensor_tensor(red_flat, turns_flat, -c2, red_flat, ALU.mult, ALU.add))
                    chain(dve.scalar_tensor_tensor(red_flat, turns_flat, -c3, red_flat, ALU.mult, ALU.add))
                if idx == 8:
                    chain(dve.tensor_scalar(red[:, 0], red[:, 0], 0.25 * TWO_PI, None, ALU.add))
                    dve.tensor_scalar(red_flat, red_flat, LIM, -LIM, ALU.min, ALU.max).then_inc(angles, 1)

            inits = [0.8 - 0.6 * math.exp(-0.3 * l) for l, (kind, _) in enumerate(LAYERS) if kind == "da"]
            dve.wait_ge(full["sc_1"], 1)
            dve.tensor_copy(gcol[:, 0:70], sc[1][:, 0:70]).then_inc(free["sc_1"], 1)
            dve.wait_ge(free["sc_1"], 1)

            def start_up(idx):
                if idx in (1, 3, 5):
                    x_turned_lo(-1, idx // 2 + 1)
                angles_step(idx)
                if idx == 9:
                    sum_squares(-1)
                if idx == 9:
                    dve.wait_ge(consts, 6)
                    dve.wait_ge(tables, 4)
                    own.step(dve.tensor_scalar(sin_a[:, :, 0, :], sin_a[:, :, 1, :], -1.0, None, ALU.mult))
                    chain(dve.tensor_scalar(sin_b[:, :, 0, :], sin_b[:, :, 1, :], -1.0, None, ALU.mult))
                if idx == 13:
                    lam_in = scr_flat[:, 0:1024].rearrange("p (l a n) -> p l a n", l=2, a=4)
                    prod = scr_flat[:, 1024:1024 + P]
                    for j in range(2):
                        for h in range(2):
                            op = dve.tensor_tensor_reduce(prod, lam_in[:, j, 2 * h, :], lam_in[:, j, 2 * h + 1, :], 1.0, 0.0,
                                                          ALU.mult, ALU.add, lam_s[:, j, h:h + 1])
                            if j + h < 2:
                                chain(op)
                            else:
                                op.then_inc(angles, 1)
                if idx == 15:
                    for j, init in enumerate(inits):
                        cols = gcol[:, NL * KC + 2 * j:NL * KC + 2 * j + 2]
                        chain(dve.tensor_scalar(cols, cols, 1.0 - init, None, ALU.mult))
                    dve.wait_ge(tables, 5)
                    for j, init in enumerate(inits):
                        chain(dve.tensor_tensor(lam[:, j:j + 1], lam_s[:, j, 0:1], lam_s[:, j, 1:2], ALU.subtract))
                        chain(dve.tensor_scalar(lam[:, j:j + 1], lam[:, j:j + 1], init, None, ALU.add))
                if idx == 16:
                    own.step(dve.tensor_scalar(sinks[:], sinks[:], -1.0, None, ALU.mult))
                    dve.wait_ge(tables, 6)
                    chain(dve.tensor_tensor(wg_lo[:], wg_raw[:], wg_hi[:].bitcast(F32), ALU.subtract))

            def turned_lo(dst_lo, dst_hi, b, name, index, cols, hi_at):
                dve.wait_ge(full[name], index + 1)
                dve.wait_ge(sig["t_hi"], hi_at + 2)
                for c2 in range(2):
                    src = tp[b][:, S * c2:S * c2 + S]
                    col = cols[c2]
                    op = dve.scalar_tensor_tensor(dst_lo(2 * b + c2), src, 1.0 if col is None else col,
                                                  dst_hi(2 * b + c2), ALU.mult, ALU.subtract)
                    if c2 == 1:
                        op.then_inc(free[name], 1)

            def x_turned_lo(l, n):
                if l == NL - 1:
                    return
                for b in range(2):
                    at = KC * (l + 1) + 4 * n + 2 * b
                    turned_lo(lambda c: xt_lo[:, 4 * n + c, :], lambda c: xt_hi[:, 4 * n + c, :].bitcast(F32), b, f"tp_{b}",
                              in_out(l, f"tp_{b}", n), [gcol[:, at + c2:at + c2 + 1] for c2 in range(2)],
                              in_out(l, "t_hi", 4 * n + 2 * b))

            def o_turned_lo(l, i, b, index, nth):
                pick = lambda buf, c: buf[:, bass.ds(4 * i + c, 1), :].rearrange("p a n -> p (a n)")
                turned_lo(lambda c: pick(ot_lo, c), lambda c: pick(ot_hi[:].bitcast(F32), c), b, f"tp_{b}", index,
                          [scale_col(l, 0), scale_col(l, 1)], in_iter(l, "t_hi", i, 2 * nth))

            def sum_squares(l):
                dve.wait_ge(sig["x_sq"], in_out(l, "x_sq", 8))
                dve.tensor_reduce(x_sum[:], x_ss[:], AX_X, ALU.add).then_inc(x_summed, 1)

            x_turned_lo(-1, 0)

            def take(dst, name, b_ap, index):
                dve.wait_ge(full[name], index + 1)
                dve.tensor_copy(dst, b_ap).then_inc(free[name], 1)

            def rope(buf, t, heads, half, cos, sin, width, before):
                if not isinstance(before, int) or before > 0:
                    dve.wait_ge(sig["roped"], before)
                xv = buf[:, t, 0:width].rearrange("p (h a n) -> p h a n", h=heads, a=2)
                a = rope_a[:, 0:width].rearrange("p (h a n) -> p h a n", h=heads, a=2)
                b = rope_b[:, 0:width].rearrange("p (h a n) -> p h a n", h=heads, a=2)
                c = cos[:, t, :].unsqueeze(1).unsqueeze(1).to_broadcast([P, heads, 2, half])
                own.step(dve.tensor_tensor(a, xv, c, ALU.mult))
                for side in range(2):
                    s = sin[:, t, side, :].unsqueeze(1).to_broadcast([P, heads, half])
                    own.step(dve.tensor_tensor(b[:, :, side, :], xv[:, :, 1 - side, :], s, ALU.mult))
                own.wait()
                dve.tensor_tensor(buf[:, t, 0:width], rope_a[:, 0:width], rope_b[:, 0:width], ALU.add)\
                   .then_inc(sig["roped"], 1)

            def row_maxima(l, i, m, slot, bank, index, mask):
                kind = LAYERS[l][0]
                name = f"sc_{bank}"
                dve.wait_ge(full[name], index + 1)
                dve.sem_inc(scores_seen)
                s = sc[bank]
                own.step(dve.tensor_tensor_reduce(scr[:, slot, 0:P], s[:, 0:P], mask_causal, 1.0, -3e38, ALU.add,
                                                  ALU.max, row_max[:, slot, 0:1]))
                dve.tensor_tensor_reduce(scr[:, slot, P:BLK], s[:, P:BLK], mask, 1.0, -3e38, ALU.add,
                                         ALU.max, row_max[:, slot, 1:2]).then_inc(free[name], 1)
                own.wait()
                dve.wait_ge(free[name], index + 1)
                if kind == "da":
                    op = dve.tensor_scalar(neg_max_t[:, slot, :], row_max[:, slot, :], -(128 ** -0.5), None, ALU.mult)
                else:
                    op = dve.tensor_scalar(neg_max_t[:, slot, :], row_max[:, slot, :], -(64 ** -0.5),
                                           sink_cur[:, slot:slot + 1], ALU.mult, ALU.min)
                op.then_inc(sig["neg_max"], 1)

            def gate(l, J, i, b, base_ap=None):
                dve.wait_ge(pairs_done, PAIRS * (J + 1))
                for t in range(T):
                    if base_ap is None:
                        dve.wait_ge(sig["tanh_done"], in_iter(l, "tanh_done", i, t + 1))
                        own.step(dve.tensor_scalar(th[:, t, :], th[:, t, :], 1.0, 0.5, ALU.add, ALU.mult))
                    else:
                        own.step(dve.tensor_scalar(base_ap[:, t, :], base_ap[:, t, :], 1.0, 0.25, ALU.add, ALU.mult))
                        own.wait()
                        dve.wait_ge(sig["tanh_done"], in_iter(l, "tanh_done", i, t + 1))
                        own.step(dve.scalar_tensor_tensor(th[:, t, :], th[:, t, :], 1.0, base_ap[:, t, :], ALU.add, ALU.mult))
                own.wait()
                for t in range(T):
                    dve.scalar_tensor_tensor(gs[:, t, :], acc[b][t][:], rstd[:, t:t + 1], th[:, t, :], ALU.mult, ALU.mult)\
                       .then_inc(dve_emptied, 1)

            def mix(l, i, factors):
                wait_emptied(dve, l, LOOP0[l] + 3, i)
                for h in range(2):
                    for t in range(T):
                        part = gs[:, t, S * h:S * h + S]
                        if LAYERS[l][0] == "ml":
                            dve.scalar_tensor_tensor(part, ml_values(h, t)[:, 0:S], factors[:, h, t:t + 1], part,
                                                     ALU.mult, ALU.mult).then_inc(free[f"tp_{h}" if t else f"sc_{h}"], 1)
                            continue
                        op = dve.scalar_tensor_tensor(part, sc[h][:, S * t:S * t + S], factors[:, h, t:t + 1], part,
                                                      ALU.mult, ALU.mult)
                        if t == 1:
                            op.then_inc(free[f"sc_{h}"], 1)

            def side_da(w, l):
                n_da = LAYERS[l][1]
                par = LOOP0[l] % 2
                for t in range(T):
                    if (i := w.due(DA["q_evac"] + t)) is not None:
                        wait_emptied(dve, l, LOOP0[l], i)
                        rope(qs, t, 4, 64, cos_a, sin_a, JW, in_iter(l, "roped", i, t))
                    if (i := w.due(DA["k_evac"] + t)) is not None:
                        wait_emptied(dve, l, LOOP0[l] + 1, i)
                        rope(ks, t, 4, 64, cos_a, sin_a, JW, in_iter(l, "roped", i, 2 + t))
                if (i := w.due(DA["q_copy"])) is not None:
                    take(qT[:, 2:4, :], "tp_1", tp[1][:], in_iter(l, "tp_1", i, 0))
                if (i := w.due(DA["k_copy"])) is not None:
                    take(kT[:, 2:4, :], "tp_1", tp[1][:], in_iter(l, "tp_1", i, 1))
                for m in range(4):
                    if (i := w.due(DA["softmax"] + m)) is not None:
                        row_maxima(l, i, m, m, m % 2, in_iter(l, f"sc_{m % 2}", i, m // 2), mask_da)
                for h in range(2):
                    if (i := w.due(DA["diff"][h])) is not None:
                        dve.wait_ge(sig["exp_done"], in_iter(l, "exp_done", i, 4 * h + 4))
                        chain(dve.reciprocal(exp_inv[:, 2 * h:2 * h + 2, :], exp_sum[:, 2 * h:2 * h + 2, :]))
                        chain(dve.tensor_scalar(exp_inv[:, 2 * h + 1, :], exp_inv[:, 2 * h + 1, :], lam[:, n_da:n_da + 1],
                                                None, ALU.mult))
                        blocks = (slice(0, P), slice(P, BLK))
                        for t, c in enumerate(blocks):
                            e1 = scr[:, 2 * h + 1, c]
                            own.step(dve.tensor_scalar(e1, e1, exp_inv[:, 2 * h + 1, t:t + 1], None, ALU.mult))
                        own.wait()
                        for t, c in enumerate(blocks):
                            dve.scalar_tensor_tensor(scr[:, 2 * h, c], scr[:, 2 * h, c], exp_inv[:, 2 * h, t:t + 1],
                                                     scr[:, 2 * h + 1, c], ALU.mult, ALU.subtract)\
                               .then_inc(sig["diff_done"], 1)
                if (i := w.due(DA["p_copy"][1])) is not None:
                    take(pT[:, 1, :], "tp_1", tp[1][:, 0:BLK], in_iter(l, "tp_1", i, 2))
                if (i := w.due(DA["gate"])) is not None:
                    gate(l, LOOP0[l] + 4 * i + 3, i, 1 - par)
                if (i := w.due(DA["mix"])) is not None:
                    dve.wait_ge(sig["o_rstd"], in_iter(l, "o_rstd", i, 2))
                    mix(l, i, o_rs)
                if (i := w.due(DA["o_split"])) is not None:
                    for b in range(2):
                        o_turned_lo(l, i, b, in_iter(l, f"tp_{b}", i, 3), b)

            def side_sw(w, l):
                par = LOOP0[l] % 2
                for t in range(T):
                    if w.phase == "iter" and w.first and w.idx == SW["kv_evac"] + 1 + t:
                        wait_emptied(dve, l, JOB0[l])
                        rope(ks, t, 4, 32, cos_b, sin_b, S, in_head(l, "roped", t))
                    if (i := w.due(SW["q_evac"] + t)) is not None:
                        wait_emptied(dve, l, LOOP0[l], i)
                        rope(qs, t, 8, 32, cos_b, sin_b, JW, in_iter(l, "roped", i, t))
                if (i := w.due(SW["k_stage"])) is not None:
                    dve.wait_ge(sig["roped"], in_head(l, "roped", 2))
                    for a in range(2):
                        own.step(dve.tensor_copy(k_stage[:, :, a, :], ks[:, :, bass.ds(64 * i, 64)]))
                    dve.tensor_copy(sink_cur[:], sinks[:, bass.ds(8 * i, 8)]).then_inc(sig["k_staged"], 1)
                if (i := w.due(SW["v_stage"])) is not None:
                    dve.tensor_copy(v_stage[:], ks[:, :, bass.ds(64 * i + S, 64)]).then_inc(sig["v_staged"], 1)
                if (i := w.due(SW["q_copy"])) is not None:
                    take(qT[:, 2:4, :], "tp_1", tp[1][:], in_iter(l, "tp_1", i, 0))
                for g in range(2):
                    four = slice(4 * g, 4 * g + 4)
                    if (i := w.due(SW["den"][g])) is not None:
                        dve.wait_ge(sig["sink_exp"], in_iter(l, "sink_exp", i, g + 1))
                        dve.wait_ge(sig["exp_done"], in_iter(l, "exp_done", i, 8 * g + 8))
                        chain(dve.tensor_tensor(exp_sum[:, four, :], exp_sum[:, four, :], sink_t[:, four, :], ALU.add))
                        own.step(dve.reciprocal(exp_inv[:, four, :], exp_sum[:, four, :]))
                for g in range(2):
                    if (i := w.due(SW["mix"][g])) is not None:
                        four = slice(4 * g, 4 * g + 4)
                        wait_emptied(dve, l, LOOP0[l] + 1, i)
                        dve.wait_ge(full["sc_1"], in_iter(l, "sc_1", i, 2 + g))
                        own.wait()
                        for t in range(T):
                            o = sc[1][:, S * t:S * t + S].rearrange("p (h n) -> p h n", h=4)
                            tmp = th[:, t, S * g:S * g + S]
                            inv = exp_inv[:, four, t:t + 1].to_broadcast([P, 4, 64])
                            own.step(dve.tensor_tensor(tmp.rearrange("p (h n) -> p h n", h=4), o, inv, ALU.mult))
                        own.wait()
                        for t in range(T):
                            part = gs[:, t, S * g:S * g + S]
                            op = dve.tensor_tensor(part, part, th[:, t, S * g:S * g + S], ALU.mult)
                            if t == 1:
                                op.then_inc(free["sc_1"], 1)
                for b in range(2):
                    if (i := w.due(SW["o_split"][b])) is not None:
                        o_turned_lo(l, i, b, in_iter(l, f"tp_{b}", i, 5), b)
                for h in range(8):
                    if (i := w.due(SW["softmax"] + h)) is not None:
                        if h == 0:
                            dve.wait_ge(sig["k_staged"], in_iter(l, "k_staged", i, 1))
                        row_maxima(l, i, h, h, 0, in_iter(l, "sc_0", i, h), mask_sw)
                    if h % 2 and (i := w.due(SW["p_copy"] + h)) is not None:
                        take(pT[:, 1, :], "tp_1", tp[1][:, 0:BLK], in_iter(l, "tp_1", i, 1 + h // 2))
                for g in range(2):
                    four = slice(4 * g, 4 * g + 4)
                    if (i := w.due(SW["sink"][g])) is not None:
                        dve.wait_ge(sig["neg_max"], in_iter(l, "neg_max", i, 4 * g + 4))
                        minus = sink_cur[:, four].unsqueeze(2).to_broadcast([P, 4, T])
                        dve.tensor_tensor(sink_t[:, four, :], neg_max_t[:, four, :], minus, ALU.subtract)\
                           .then_inc(sig["sink_arg"], 1)
                if (i := w.due(SW["gate"])) is not None:
                    gate(l, LOOP0[l] + 2 * i + 1, i, 1 - par)

            def gates(w, l):
                if w.idx == 8:
                    chain(dve.memset(vs_row[:, 0:2 * RUN], -3e38))
                if w.idx == 7:
                    dve.wait_ge(full["tp_0"], in_head(l, "tp_0", 1))
                    dve.tensor_copy(gate_rows, tp[0][0:16, 0:S]).then_inc(free["tp_0"], 1)
                if w.idx == 9:
                    dve.wait_ge(full["tp_1"], in_head(l, "tp_1", 1))
                    dve.wait_ge(rstd_ready, 2 * l + 2)
                    own.step(dve.scalar_tensor_tensor(gz[:, 0, :], tp[1][:, 0:16], rstd[:, 0:1], gbias[:], ALU.mult, ALU.add))
                    dve.scalar_tensor_tensor(gz[:, 1, :], tp[1][:, 16:32], rstd[:, 1:2], gbias[:], ALU.mult, ALU.add)\
                       .then_inc(free["tp_1"], 1)
                    own.wait()
                    dve.wait_ge(free["tp_1"], in_head(l, "tp_1", 1))
                    z = gz[:, :, 8:16]
                    dve.scalar_tensor_tensor(lf_a[:], z, -1.0, z, ALU.mult, ALU.min).then_inc(gate_dve, 1)
                if w.idx == 10:
                    dve.wait_ge(gate_act, 1)
                    dve.tensor_scalar(lf_u[:], lf_e[:], 1.0, None, ALU.add).then_inc(gate_dve, 1)
                    dve.wait_ge(gate_dve, 2)
                    chain(dve.scalar_tensor_tensor(lf[:], lf_u[:], -1.0, lf_e[:], ALU.add, ALU.subtract))
                    chain(dve.reciprocal(lf_a[:], lf_u[:]))
                    chain(dve.tensor_tensor(lf[:], lf[:], lf_a[:], ALU.mult))
                    dve.wait_ge(gate_act, 2)
                    chain(dve.tensor_tensor(lf[:], lf[:], lf_l[:], ALU.subtract))
                    dve.scalar_tensor_tensor(lf[:], gz[:, :, 8:16], 0.0, lf[:], ALU.min, ALU.add).then_inc(gate_dve, 1)
                if w.idx == 12:
                    dve.wait_ge(full["tp_1"], in_head(l, "tp_1", 2))
                    dve.tensor_copy(F_t[:].rearrange("p a b -> p (a b)"), tp[1][:, 0:24]).then_inc(free["tp_1"], 1)
                    dve.wait_ge(free["tp_1"], in_head(l, "tp_1", 2))
                    own.step(dve.tensor_tensor(rcol[:, 2, :], gz[:, 1, 0:8], F_t[:, 1, :], ALU.subtract))
                    chain(dve.tensor_tensor(rcol[:, 0, :], gz[:, 0, 0:8], F_t[:, 0, :], ALU.subtract))
                    dve.tensor_tensor(rcol[:, 1, :], rcol[:, 0, :], F_t[:, 2, :], ALU.add).then_inc(gate_dve, 1)
                if w.idx == 14:
                    dve.wait_ge(full["tp_0"], in_head(l, "tp_0", 2))
                    r = tp[0][0:8, :].rearrange("p (a t n) -> p a t n", a=2, t=T)
                    own.step(dve.tensor_copy(run_a[:, :, PAD:PAD + P], r[:, 0]))
                    dve.tensor_copy(F_r[:], r[:, 1]).then_inc(free["tp_0"], 1)
                    dve.wait_ge(free["tp_0"], in_head(l, "tp_0", 2))
                    own.wait()
                for n in range(7):
                    if w.idx == 14 + n // 4:
                        step = 2 ** n
                        src, dst = (run_a, run_b) if n % 2 == 0 else (run_b, run_a)
                        chain(dve.tensor_tensor(dst[:, :, PAD:PAD + P], src[:, :, PAD:PAD + P],
                                                src[:, :, PAD - step:PAD - step + P], ALU.max))
                if w.idx == 20:
                    dve.wait_ge(free["sc_1"], in_head(l, "sc_1", 2))
                    dve.memset(v_ones[:, :, :, S:VW], 1.0).then_inc(gate_dve, 1)
                if w.idx == 15:
                    src, dst = run_b, run_a
                    chain(dve.tensor_scalar(dst[:, 0, PAD:PAD + P], src[:, 0, PAD:PAD + P], 0.0, None, ALU.max))
                    chain(dve.tensor_tensor(m_end[:], dst[:, 0, PAD + P - 1:PAD + P], F_r[:, 0, P - 1:P], ALU.add))
                    chain(dve.tensor_scalar(dst[:, 1, PAD:PAD + P], src[:, 1, PAD:PAD + P], m_end[:, 0:1], None, ALU.max))
                    dve.tensor_tensor(m_r[:], dst[:, :, PAD:PAD + P], F_r[:], ALU.add).then_inc(gate_dve, 1)

            to_view = scr_flat[:, 4 * BLK:4 * BLK + T * JW].rearrange("p (t n) -> p t n", t=T)

            def side_ml(w, l):
                par = LOOP0[l] % 2
                if w.phase == "iter" and w.first:
                    gates(w, l)
                if (i := w.due(ML["qk_copy"])) is not None:
                    take(kT[:, 0:2, :], "tp_1", tp[1][:], in_iter(l, "tp_1", i, 0))
                for h in range(2):
                    if (i := w.due(ML["decay"][h])) is not None:
                        if w.first:
                            dve.wait_ge(free[f"sc_{h}"], in_head(l, f"sc_{h}", 1))
                            dve.wait_ge(gate_dve, 4)
                        else:
                            for b in range(2):
                                dve.wait_ge(free[f"sc_{b}"], in_head(l, f"sc_{b}", 2))
                        head = 2 * i + h
                        for c, (t, mask) in enumerate(((0, mask_ml), (1, None), (1, mask_ml))):
                            m_t = wide[:, bass.ds(head, 1), P * t:P * t + P].rearrange("p a n -> p (a n)")
                            r = rcol[:, c, bass.ds(head, 1)]
                            d = scr[:, h, P * c:P * c + P]
                            if mask is None:
                                op = dve.tensor_scalar(d, m_t, r, 0.0, ALU.subtract, ALU.max)
                            else:
                                op = dve.scalar_tensor_tensor(d, m_t, r, mask[:], ALU.subtract, ALU.max)
                            if c == 2:
                                op.then_inc(sig["decay_arg"], 1)
                    if (i := w.due(ML["weigh"][h])) is not None:
                        dve.wait_ge(full[f"sc_{h}"], in_iter(l, f"sc_{h}", i, 1))
                        dve.wait_ge(sig["exp_done"], in_iter(l, "exp_done", i, h + 1))
                        dve.scalar_tensor_tensor(scr[:, 2 + h, :], sc[h][:, 0:BLK], 128 ** -0.5, scr[:, h, :],
                                                 ALU.mult, ALU.mult).then_inc(free[f"sc_{h}"], 1)
                if (i := w.due(ML["den"])) is not None:
                    for h in range(2):
                        dve.wait_ge(full[f"sc_{h}"], in_iter(l, f"sc_{h}", i, 2))
                        dve.wait_ge(full[f"tp_{h}"], in_iter(l, f"tp_{h}", i, 2))
                        for t in range(T):
                            own.step(dve.tensor_copy(den_s[:, h, t:t + 1], ml_values(h, t)[:, S:VW]))
                    own.wait()
                    chain(dve.scalar_tensor_tensor(den_i[:], den_s[:], -1.0, den_s[:], ALU.mult, ALU.max))
                    e = exp_nm[:, :, bass.ds(2 * i, 2)].rearrange("p t h -> p h t")
                    chain(dve.tensor_tensor(den_s[:], den_i[:], e, ALU.max))
                    dve.reciprocal(den_i[:], den_s[:]).then_inc(sig["den_inv"], 1)
                if (i := w.due(ML["comb"])) is not None:
                    dve.wait_ge(sig["o_rstd"], in_iter(l, "o_rstd", i, 1))
                    dve.wait_ge(sig["den_inv"], in_iter(l, "den_inv", i, 1))
                    own.step(dve.tensor_tensor(comb[:], den_i[:], o_rs[:], ALU.mult))
                if (i := w.due(ML["gate"])) is not None:
                    wait_emptied(dve, l, LOOP0[l] + 2, i)
                    gate(l, LOOP0[l] + 4 * i + 3, i, 1 - par, to_view)
                if (i := w.due(ML["mix"])) is not None:
                    own.wait()
                    mix(l, i, comb)
                if (i := w.due(ML["o_split"])) is not None:
                    o_turned_lo(l, i, 0, in_iter(l, "tp_0", i, 2), 0)
                    o_turned_lo(l, i, 1, in_iter(l, "tp_1", i, 2), 1)

            sides = {"da": side_da, "sw": side_sw, "ml": side_ml}

            def final_gain(n):
                dve.wait_ge(final_in, 16)
                dve.wait_ge(sig["x_sq"], in_out(NL - 1, "x_sq", 2 * n + 2))
                for t in range(T):
                    part = xres[:, t, JW * n:JW * n + JW]
                    dve.tensor_tensor(part, part, shared[:, JW * n:JW * n + JW], ALU.mult).then_inc(y_gained, 1)

            def add_residual(l, n):
                b = (OUT0[l] + n) % 2
                dve.wait_ge(pairs_done, PAIRS * OUT0[l] + X_END[n])
                for t in range(T):
                    part = xres[:, t, JW * n:JW * n + JW]
                    dve.tensor_tensor(part, part, acc[b][t][:], ALU.add).then_inc(dve_emptied, 1)

            def pair(w, j0, i, j, p):
                J = j0 + ITER_JOBS[w.kind] * i
                if (ln := w.x_due(X_SUM)) is not None:
                    add_residual(*ln)
                if (ln := w.x_due(X_SPLIT)) is not None:
                    x_turned_lo(*ln)
                    if ln[1] == OUT_JOBS - 1:
                        sum_squares(ln[0])
                    if ln[0] == NL - 1:
                        final_gain(ln[1])
                sides[w.kind](w, w.l)
                dve.wait_ge(hi_ready, PAIRS * J + p + 1)
                q = 2 * (p % LAG)
                dve.tensor_tensor(w_lo[:, q:q + 2, :], raw[:, 2 * p:2 * p + 2, :], w_hi[:, q:q + 2, :].bitcast(F32),
                                  ALU.subtract).then_inc(lo_ready, 1)
                if w.start:
                    start_up(w.idx)

            for l in range(NL):
                walk(dve, l, pair, own, "dve")
            last = OUT_JOBS - 1
            dve.wait_ge(y_gained, T * last)
            for t in range(T):
                dve.wait_ge(tiles_done, t + 1)
                part = xres[:, t, JW * last:JW * last + JW]
                dve.tensor_tensor(part, part, acc[J0_LAST % 2][t][:], ALU.add).then_inc(dve_emptied, 1)
                dve.wait_ge(dve_emptied, emptied(NL - 1, NJOBS - 1)[1] - T + t + 1)
                own.step(dve.tensor_tensor(qs[:, t, :], part, shared[:, JW * last:JW * last + JW], ALU.mult))
                dve.wait_ge(sig["x_sq"], in_out(NL - 1, "x_sq", 2 * last + t + 1))
                dve.tensor_reduce(x_sum[:, t:t + 1], x_ss[:, t, :], AX_X, ALU.add).then_inc(x_summed, 1)
                own.wait()
                dve.wait_ge(rstd_ready, 2 * NL + t + 1)
                for part in (qs[:, t, :], xres[:, t, 0:JW], xres[:, t, JW:2 * JW]):
                    dve.tensor_scalar(part, part, rstd[:, t:t + 1], None, ALU.mult).then_inc(y_ready, 1)


_INS = ["x", "positions", "norm_g", "final_g", "da_w_in", "da_w_out", "da_lambda", "da_subln_g", "sw_w_in", "sw_w_out",
        "sw_sinks", "ml_w_in", "ml_b_gates", "ml_w_out", "ml_norm_g"]


def kernel(**inputs):
    import numpy as _np
    import concourse.bacc as _bacc
    from concourse import mybir as _mybir
    from concourse.bass_utils import run_bass_kernel_spmd as _run

    nc = _bacc.Bacc("TRN2", target_bir_lowering=False, num_devices=1)
    arrays, args = {}, []
    given = {name: _np.ascontiguousarray(inputs[name]) for name in _INS}
    given["freqs"] = _np.concatenate([THETA ** (-_np.arange(0, d, 2, dtype=_np.float64) / d) for d in (128, 64)])\
                        .astype(_np.float32)
    for name, a in given.items():
        arrays[f"in_{name}_dram"] = a
        args.append(nc.dram_tensor(f"in_{name}_dram", a.shape, _mybir.dt.from_np(a.dtype), kind="ExternalInput").ap())
    args.append(nc.dram_tensor("out_0_dram", (1, S, D), F32, kind="ExternalOutput").ap())
    build(nc, *args)
    r = _run(nc, [arrays], core_ids=[0])
    return r.results[0]["out_0_dram"]
```
